# Optimizing a Trainium2 kernel written in Bass

```python
import math
import jax, jax.numpy as jnp
from jax import lax
import numpy as np

D_MODEL = 1024
BATCH = 1
SEQ = 256
DEPTH = 1

GRID_W = 64
CTX_LEN = 256
N_HEADS = 8
HEAD_DIM = 128
D_GDN = N_HEADS * HEAD_DIM
CONV_K = 5
GDN_CHUNK = 64
SGU_GROUPS = 8
SGU_GROUP_DIM = 128
D_SGU = SGU_GROUPS * SGU_GROUP_DIM
SGU_CHUNK = 128
ROWS_PER_CHUNK = SGU_CHUNK // GRID_W
N_EXPERT_GROUPS = 4
EXPERTS_PER_GROUP = 8
N_EXPERTS = N_EXPERT_GROUPS * EXPERTS_PER_GROUP
TOP_K = 2
D_EXPERT = 256
N_MOD = 6
EPS = 1e-6
COL_BETA = 3 * D_GDN
COL_A = COL_BETA + 2 * N_HEADS
COL_Z = COL_A + 2 * N_HEADS
COL_U = COL_Z + D_GDN
COL_V = COL_U + D_SGU
COL_GATE = COL_V + D_SGU
D_IN = COL_GATE + 2 * D_MODEL


def rms_norm(x, gain):
    xf = x.astype(jnp.float32)
    y = xf * lax.rsqrt(jnp.mean(xf * xf, axis=-1, keepdims=True) + EPS)
    return (y * gain.astype(jnp.float32)).astype(x.dtype)

def layer_norm(x, gain, bias):
    xf = x.astype(jnp.float32)
    mu = jnp.mean(xf, axis=-1, keepdims=True)
    var = jnp.mean(jnp.square(xf - mu), axis=-1, keepdims=True)
    y = (xf - mu) * lax.rsqrt(var + EPS)
    return (y * gain.astype(jnp.float32) + bias.astype(jnp.float32)).astype(x.dtype)

def l2_normalize(t):
    return t * lax.rsqrt(jnp.sum(t * t, axis=-1, keepdims=True) + EPS)

def modulate(h, shift, scale):
    return h * (1.0 + scale[:, None, :]) + shift[:, None, :]

def adaln_params(cond, w, b):
    m = jax.nn.silu(cond) @ w + b
    return m.reshape(cond.shape[0], N_MOD, D_MODEL)

def centred_depthwise_conv(x, w):
    C = x.shape[-1]
    pad = CONV_K // 2
    return lax.conv_general_dilated(
        x, w.reshape(CONV_K, 1, C).astype(x.dtype), window_strides=(1,), padding=((pad, pad),),
        dimension_numbers=('NWC', 'WIO', 'NWC'), feature_group_count=C)

def gated_delta_chunked(q, k, v, g, beta, s0):
    B, H, L, dk = q.shape
    n = L // GDN_CHUNK
    C = GDN_CHUNK
    rs = lambda t: t.reshape(B, H, n, C, *t.shape[3:])
    q, k, v, g, beta = rs(q), rs(k), rs(v), rs(g), rs(beta)
    G = jnp.cumsum(g, axis=-1)
    incl = jnp.tril(jnp.ones((C, C), dtype=bool))
    strict = jnp.tril(jnp.ones((C, C), dtype=bool), -1)
    decay = jnp.exp(jnp.where(incl, G[..., :, None] - G[..., None, :], -jnp.inf))
    kb = k * beta[..., None]
    low = jnp.where(strict, jnp.einsum('bhncd,bhnsd->bhncs', kb, k) * decay, 0.0)
    eye = jnp.eye(C, dtype=q.dtype)
    T = lax.linalg.triangular_solve(eye + low, jnp.broadcast_to(eye, low.shape), left_side=True, lower=True)
    u = T @ (v * beta[..., None])
    w = T @ (kb * jnp.exp(G)[..., None])
    qk_intra = jnp.einsum('bhncd,bhnsd->bhncs', q, k) * decay
    q_dec = q * jnp.exp(G)[..., None]
    k_dec = k * jnp.exp(G[..., -1:] - G)[..., None]
    g_last = jnp.exp(G[..., -1])

    def step(s, inp):
        u_c, w_c, qk_c, qd_c, kd_c, gl_c = inp
        v_new = u_c - w_c @ s
        o_c = qd_c @ s + qk_c @ v_new
        s = s * gl_c[..., None, None] + jnp.swapaxes(kd_c, -1, -2) @ v_new
        return s, o_c

    xs = tuple(jnp.moveaxis(t, 2, 0) for t in (u, w, qk_intra, q_dec, k_dec, g_last))
    s_final, o = lax.scan(step, s0, xs)
    o = jnp.moveaxis(o, 0, 2).reshape(B, H, L, v.shape[-1])
    return o, s_final

def gdn_scan(p_qkv, p_beta, p_a, conv_w, a_log, dt_bias, s_init):
    B, L, _ = p_qkv.shape
    qkv = jax.nn.silu(centred_depthwise_conv(p_qkv, conv_w)).astype(jnp.float32)
    heads = lambda t: jnp.swapaxes(t.reshape(B, L, N_HEADS, HEAD_DIM), 1, 2)
    q, k, v = (heads(t) for t in jnp.split(qkv, 3, axis=-1))
    q = l2_normalize(q) * (HEAD_DIM ** -0.5)
    k = l2_normalize(k)
    dirs = lambda t: t.astype(jnp.float32).reshape(B, L, 2, N_HEADS).transpose(2, 0, 3, 1)
    beta = jax.nn.sigmoid(dirs(p_beta))
    g = -jnp.exp(a_log.astype(jnp.float32))[:, None, :, None] * jax.nn.softplus(
        dirs(p_a) + dt_bias.astype(jnp.float32)[:, None, :, None])
    o_f, s_f = gated_delta_chunked(q, k, v, g[0], beta[0], s_init[0])
    flip = lambda t: jnp.flip(t, axis=2)
    o_b, s_b = gated_delta_chunked(flip(q), flip(k), flip(v), flip(g[1]), flip(beta[1]), s_init[1])
    o = jnp.swapaxes(o_f + flip(o_b), 1, 2)
    return o, jnp.stack([s_f, s_b])

def gdn_output(o, p_z, norm_g):
    B, L = o.shape[:2]
    z = p_z.astype(jnp.float32).reshape(B, L, N_HEADS, HEAD_DIM)
    y = rms_norm(o, norm_g) * jax.nn.silu(z)
    return y.reshape(B, L, D_GDN).astype(p_z.dtype)

def sgu_mixer(p_u, p_v, n_chunks, ln_g, ln_b, w_s, b_s):
    B, L, _ = p_u.shape
    u = jax.nn.gelu(p_u)
    v = layer_norm(jax.nn.gelu(p_v), ln_g, ln_b).reshape(B, n_chunks, SGU_CHUNK, SGU_GROUPS, SGU_GROUP_DIM)
    mixed = jnp.einsum('gpq,bnqgc->bnpgc', w_s, v) + b_s.T[:, :, None]
    return u * mixed.reshape(B, L, D_SGU)

def merge_branches(y_gdn, y_sgu, p_gates, w_a, w_b, w_o):
    g_a, g_b = jnp.split(jax.nn.sigmoid(p_gates), 2, axis=-1)
    return (g_a * (y_gdn @ w_a) + g_b * (y_sgu @ w_b)) @ w_o

def hier_moe(h, w_rg, b_rg, w_re, b_re, w1, w3, w2):
    B, L, D = h.shape
    t = h.reshape(B * L, D)
    p_group = jax.nn.softmax((t @ w_rg + b_rg).astype(jnp.float32), axis=-1)
    grp = jnp.argmax(p_group, axis=-1)
    p_g = jnp.take_along_axis(p_group, grp[:, None], axis=-1)
    logits_e = (t @ w_re + b_re).astype(jnp.float32).reshape(-1, N_EXPERT_GROUPS, EXPERTS_PER_GROUP)
    logits_in = jnp.take_along_axis(logits_e, grp[:, None, None], axis=1)[:, 0]
    top_p, top_i = lax.top_k(jax.nn.softmax(logits_in, axis=-1), TOP_K)
    top_p = top_p / jnp.sum(top_p, axis=-1, keepdims=True) * p_g
    expert_id = grp[:, None] * EXPERTS_PER_GROUP + top_i
    gate = jnp.sum(jax.nn.one_hot(expert_id, N_EXPERTS, dtype=jnp.float32) * top_p[..., None], axis=1)
    gate = gate.astype(h.dtype).reshape(-1, N_EXPERT_GROUPS, EXPERTS_PER_GROUP)
    out = jnp.zeros_like(t)
    for gi in range(N_EXPERT_GROUPS):
        sl = slice(gi * EXPERTS_PER_GROUP, (gi + 1) * EXPERTS_PER_GROUP)
        hid = jax.nn.silu(jnp.einsum('td,edf->tef', t, w1[sl])) * jnp.einsum('td,edf->tef', t, w3[sl])
        out = out + jnp.einsum('tef,efd->td', hid * gate[:, gi, :, None], w2[sl])
    return out.reshape(B, L, D)

def first_inputs(seed: int = 0) -> dict:
    key = jax.random.key(seed)
    ks = jax.random.split(key, 32)
    f32 = jnp.float32
    nrm = lambda k, shape, scale: jax.random.normal(k, shape, f32) * scale
    gain = lambda k, shape: 1.0 + 0.1 * jax.random.normal(k, shape, f32)
    dt = jnp.exp(jax.random.uniform(ks[9], (DEPTH, 2, N_HEADS), f32, math.log(1e-3), math.log(1e-1)))
    return {
        'x': nrm(ks[0], (BATCH, SEQ, D_MODEL), 1.0),
        'c': nrm(ks[1], (BATCH, D_MODEL), 1.0),
        'ctx': nrm(ks[2], (BATCH, CTX_LEN, D_MODEL), 1.0),
        'c_ctx': nrm(ks[3], (D_MODEL,), 1.0),
        'ada_w': nrm(ks[4], (DEPTH, D_MODEL, N_MOD * D_MODEL), 0.5 * D_MODEL ** -0.5),
        'ada_b': nrm(ks[5], (DEPTH, N_MOD * D_MODEL), 0.02),
        'norm_mix_g': gain(ks[6], (DEPTH, D_MODEL)),
        'w_in': nrm(ks[7], (DEPTH, D_MODEL, D_IN), D_MODEL ** -0.5),
        'conv_w': nrm(ks[8], (DEPTH, CONV_K, 3 * D_GDN), CONV_K ** -0.5),
        'a_log': jnp.log(jax.random.uniform(ks[10], (DEPTH, 2, N_HEADS), f32, 1.0, 16.0)),
        'dt_bias': dt + jnp.log(-jnp.expm1(-dt)),
        'gdn_norm_g': gain(ks[11], (DEPTH, HEAD_DIM)),
        'sgu_ln_g': gain(ks[12], (DEPTH, D_SGU)),
        'sgu_ln_b': nrm(ks[13], (DEPTH, D_SGU), 0.02),
        'sgu_w': nrm(ks[14], (DEPTH, SGU_GROUPS, SGU_CHUNK, SGU_CHUNK), SGU_CHUNK ** -0.5),
        'sgu_b': gain(ks[15], (DEPTH, SGU_GROUPS, SGU_CHUNK)),
        'w_branch_a': nrm(ks[16], (DEPTH, D_GDN, D_MODEL), D_GDN ** -0.5),
        'w_branch_b': nrm(ks[17], (DEPTH, D_SGU, D_MODEL), D_SGU ** -0.5),
        'w_out': nrm(ks[18], (DEPTH, D_MODEL, D_MODEL), D_MODEL ** -0.5),
        'norm_ffn_g': gain(ks[19], (DEPTH, D_MODEL)),
        'router_group_w': nrm(ks[20], (DEPTH, D_MODEL, N_EXPERT_GROUPS), D_MODEL ** -0.5),
        'router_group_b': nrm(ks[21], (DEPTH, N_EXPERT_GROUPS), 0.01),
        'router_expert_w': nrm(ks[22], (DEPTH, D_MODEL, N_EXPERTS), D_MODEL ** -0.5),
        'router_expert_b': nrm(ks[23], (DEPTH, N_EXPERTS), 0.01),
        'expert_w1': nrm(ks[24], (DEPTH, N_EXPERTS, D_MODEL, D_EXPERT), D_MODEL ** -0.5),
        'expert_w3': nrm(ks[25], (DEPTH, N_EXPERTS, D_MODEL, D_EXPERT), D_MODEL ** -0.5),
        'expert_w2': nrm(ks[26], (DEPTH, N_EXPERTS, D_EXPERT, D_MODEL), D_EXPERT ** -0.5),
        'final_norm_g': gain(ks[27], (D_MODEL,)),
    }

def first_block(x, c, ctx, c_ctx, ada_w, ada_b, norm_mix_g, w_in, conv_w, a_log, dt_bias, gdn_norm_g,
              sgu_ln_g, sgu_ln_b, sgu_w, sgu_b, w_branch_a, w_branch_b, w_out, norm_ffn_g,
              router_group_w, router_group_b, router_expert_w, router_expert_b,
              expert_w1, expert_w3, expert_w2, final_norm_g):
    B = x.shape[0]
    rows = x.shape[1] // GRID_W
    lat_chunks = rows // ROWS_PER_CHUNK
    ctx_chunks = ctx.shape[1] // SGU_CHUNK
    s_zero = jnp.zeros((2, B, N_HEADS, HEAD_DIM, HEAD_DIM), jnp.float32)
    for l in range(DEPTH):
        mod_x = adaln_params(c, ada_w[l], ada_b[l])
        mod_c = adaln_params(c_ctx[None, :], ada_w[l], ada_b[l])
        hc = modulate(rms_norm(ctx, norm_mix_g[l]), mod_c[:, 0], mod_c[:, 1])
        hx = modulate(rms_norm(x, norm_mix_g[l]), mod_x[:, 0], mod_x[:, 1])
        c_qkv, c_beta, c_a = jnp.split(hc @ w_in[l][:, :COL_Z], (COL_BETA, COL_A), axis=-1)
        o_c, s_ctx = gdn_scan(c_qkv, c_beta, c_a, conv_w[l], a_log[l], dt_bias[l], s_zero)
        x_qkv, x_beta, x_a, x_z, x_u, x_v, x_gates = jnp.split(
            hx @ w_in[l], (COL_BETA, COL_A, COL_Z, COL_U, COL_V, COL_GATE), axis=-1)
        o_x, _ = gdn_scan(x_qkv, x_beta, x_a, conv_w[l], a_log[l], dt_bias[l], s_ctx)
        y_gdn = gdn_output(o_x, x_z, gdn_norm_g[l])
        y_sgu = sgu_mixer(x_u, x_v, lat_chunks, sgu_ln_g[l], sgu_ln_b[l], sgu_w[l], sgu_b[l])
        x = x + mod_x[:, 2][:, None, :] * merge_branches(y_gdn, y_sgu, x_gates, w_branch_a[l], w_branch_b[l], w_out[l])
        hx = modulate(rms_norm(x, norm_ffn_g[l]), mod_x[:, 3], mod_x[:, 4])
        x = x + mod_x[:, 5][:, None, :] * hier_moe(hx, router_group_w[l], router_group_b[l], router_expert_w[l],
                                                   router_expert_b[l], expert_w1[l], expert_w3[l], expert_w2[l])
        if l < DEPTH - 1:
            c_z, c_u, c_v, c_gates = jnp.split(hc @ w_in[l][:, COL_Z:], (D_GDN, D_GDN + D_SGU, D_GDN + 2 * D_SGU), axis=-1)
            yc_gdn = gdn_output(o_c, c_z, gdn_norm_g[l])
            yc_sgu = sgu_mixer(c_u, c_v, ctx_chunks, sgu_ln_g[l], sgu_ln_b[l], sgu_w[l], sgu_b[l])
            ctx = ctx + mod_c[:, 2][:, None, :] * merge_branches(yc_gdn, yc_sgu, c_gates, w_branch_a[l], w_branch_b[l], w_out[l])
            hc = modulate(rms_norm(ctx, norm_ffn_g[l]), mod_c[:, 3], mod_c[:, 4])
            ctx = ctx + mod_c[:, 5][:, None, :] * hier_moe(hc, router_group_w[l], router_group_b[l], router_expert_w[l],
                                                           router_expert_b[l], expert_w1[l], expert_w3[l], expert_w2[l])
    return rms_norm(x, final_norm_g)


HEAD_DIM_2 = 64
N_HEADS_2 = D_MODEL // HEAD_DIM_2
N_HEADS_SB = N_HEADS_2 // 2
N_HEADS_DIL = N_HEADS_2 - N_HEADS_SB
D_SB = N_HEADS_SB * HEAD_DIM_2
D_DIL = N_HEADS_DIL * HEAD_DIM_2
DIL_PATTERNS = ((128, 1), (512, 4), (2048, 16))
BLOCK = 128
N_BUCKETS = 32
MAX_DISTANCE = 2048
N_EXPERTS_2 = 16
N_GROUPS = 4
EXPERTS_PER_GROUP_2 = N_EXPERTS_2 // N_GROUPS
D_FF_EXPERT = 1024
ALPHA = (2.0 * DEPTH) ** 0.25
BETA = (8.0 * DEPTH) ** -0.25
LN_EPS = 1e-5
NEG_INF = -1e30


def layer_norm_2(x, g, b):
    xf = x.astype(jnp.float32)
    mu = xf.mean(-1, keepdims=True)
    var = jnp.square(xf - mu).mean(-1, keepdims=True)
    return ((xf - mu) * lax.rsqrt(var + LN_EPS) * g.astype(jnp.float32) + b.astype(jnp.float32)).astype(x.dtype)

def head_rms_merge(o, g):
    b, h, s, dh = o.shape
    of = o.astype(jnp.float32)
    of = of * lax.rsqrt(jnp.mean(jnp.square(of), -1, keepdims=True) + 1e-6)
    of = of.transpose(0, 2, 1, 3).reshape(b, s, h * dh)
    return (of * g.astype(jnp.float32)).astype(o.dtype)

def t5_bucket(dist):
    max_exact = N_BUCKETS // 2
    d = jnp.maximum(dist, 0)
    large = max_exact + (jnp.log(jnp.maximum(d, 1).astype(jnp.float32) / max_exact)
                         / math.log(MAX_DISTANCE / max_exact) * (N_BUCKETS - max_exact)).astype(jnp.int32)
    large = jnp.minimum(large, N_BUCKETS - 1)
    return jnp.where(d < max_exact, d, large)

def stick_breaking_attention(q, k, v):
    b, h, s, dh = q.shape
    nb = s // BLOCK
    scale = dh ** -0.5
    qb = q.reshape(b, h, nb, BLOCK, dh).transpose(2, 0, 1, 3, 4)
    kpos = jnp.arange(s)

    def one_block(args):
        qblk, n = args
        z = jnp.einsum('bhqd,bhkd->bhqk', qblk, k).astype(jnp.float32) * scale
        qpos = n * BLOCK + jnp.arange(BLOCK)
        causal = kpos[None, :] < qpos[:, None]
        log_beta = jax.nn.log_sigmoid(z)
        log_1m = jnp.where(causal, jax.nn.log_sigmoid(-z), 0.0)
        between = lax.cumsum(log_1m, axis=3, reverse=True) - log_1m
        a = jnp.where(causal, jnp.exp(log_beta + between), 0.0)
        return jnp.einsum('bhqk,bhkd->bhqd', a.astype(v.dtype), v)

    out = lax.map(one_block, (qb, jnp.arange(nb)))
    return out.transpose(1, 2, 0, 3, 4).reshape(b, h, s, dh)

def dilated_branch(q, k, v, rel_bias, window, dilation):
    b, h, s, dh = q.shape
    span = window // dilation
    n_cls = s // dilation
    nb = -(-n_cls // BLOCK)
    pad = nb * BLOCK - n_cls

    def to_classes(t):
        t = t.reshape(b, h, n_cls, dilation, dh).transpose(0, 1, 3, 2, 4)
        t = jnp.pad(t, ((0, 0), (0, 0), (0, 0), (0, pad), (0, 0)))
        return t.reshape(b, h, dilation, nb, BLOCK, dh)

    def with_prev(t):
        prev = jnp.pad(t, ((0, 0), (0, 0), (0, 0), (1, 0), (0, 0), (0, 0)))[:, :, :, :nb]
        return jnp.concatenate([prev, t], axis=4)

    qc = to_classes(q)
    kk = with_prev(to_classes(k))
    vv = with_prev(to_classes(v))
    logits = jnp.einsum('bhrnqd,bhrnkd->bhrnqk', qc, kk).astype(jnp.float32) * dh ** -0.5

    qi = jnp.arange(BLOCK)[:, None]
    kj = jnp.arange(2 * BLOCK)[None, :]
    steps = qi + BLOCK - kj
    bias = rel_bias[t5_bucket(jnp.maximum(steps, 0) * dilation)].astype(jnp.float32)
    bias = bias.transpose(2, 0, 1)
    key_cls = (jnp.arange(nb)[:, None, None] - 1) * BLOCK + kj[None]
    valid = (steps >= 0) & (steps <= span) & (key_cls >= 0)
    logits = jnp.where(valid, logits + bias[None, :, None, None], NEG_INF)

    m = logits.max(-1, keepdims=True)
    p = jnp.exp(logits - m)
    denom = p.sum(-1, keepdims=True)
    o = jnp.einsum('bhrnqk,bhrnkd->bhrnqd', p.astype(vv.dtype), vv).astype(jnp.float32) / denom
    lse = (m + jnp.log(denom))[..., 0]

    def from_classes(t):
        t = t.reshape((b, h, dilation, nb * BLOCK) + t.shape[5:])[:, :, :, :n_cls]
        t = jnp.moveaxis(t, 2, 3)
        return t.reshape((b, h, s) + t.shape[4:])

    return from_classes(o), from_classes(lse)

def dilated_attention(q, k, v, rel_bias):
    outs, lses = [], []
    for window, dilation in DIL_PATTERNS:
        o, l = dilated_branch(q, k, v, rel_bias, window, dilation)
        outs.append(o)
        lses.append(l)
    w = jax.nn.softmax(jnp.stack(lses, 0), axis=0)
    return jnp.einsum('gbhs,gbhsd->bhsd', w, jnp.stack(outs, 0)).astype(q.dtype)

def token_mixer(x, w_in, g_sb, g_dil, w_out, rel_bias):
    b, s, _ = x.shape
    proj = jnp.einsum('bsd,de->bse', x, w_in)
    q_sb, k_sb, v_sb, q_dl, k_dl, v_dl = jnp.split(
        proj, [D_SB, 2 * D_SB, 3 * D_SB, 3 * D_SB + D_DIL, 3 * D_SB + 2 * D_DIL], axis=-1)
    to_heads = lambda t: t.reshape(b, s, -1, HEAD_DIM_2).transpose(0, 2, 1, 3)
    o_sb = stick_breaking_attention(to_heads(q_sb), to_heads(k_sb), to_heads(v_sb))
    o_dl = dilated_attention(to_heads(q_dl), to_heads(k_dl), to_heads(v_dl), rel_bias)
    y = jnp.concatenate([head_rms_merge(o_sb, g_sb), head_rms_merge(o_dl, g_dil)], axis=-1)
    return jnp.einsum('bse,ed->bsd', y, w_out)

def grouped_moe(x, w_router, b_router, w_gate, w_up, w_down):
    b, s, d = x.shape
    t = x.reshape(b * s, d)
    logits = (t @ w_router).astype(jnp.float32) + b_router.astype(jnp.float32)
    probs = jax.nn.softmax(logits, axis=-1)
    pg = probs.reshape(-1, N_GROUPS, EXPERTS_PER_GROUP_2)
    vals, idx = lax.top_k(pg, TOP_K)
    g_sel = jnp.argmax(vals.sum(-1), axis=-1)
    vals_sel = jnp.take_along_axis(vals, g_sel[:, None, None], axis=1)[:, 0]
    idx_sel = jnp.take_along_axis(idx, g_sel[:, None, None], axis=1)[:, 0]
    expert_ids = g_sel[:, None] * EXPERTS_PER_GROUP_2 + idx_sel
    gates = vals_sel / vals_sel.sum(-1, keepdims=True)
    gate_dense = (jax.nn.one_hot(expert_ids, N_EXPERTS_2, dtype=jnp.float32) * gates[..., None]).sum(1)
    y = jnp.zeros_like(t)
    for e in range(N_EXPERTS_2):
        h = jax.nn.silu(t @ w_gate[e]) * (t @ w_up[e])
        y = y + gate_dense[:, e:e + 1].astype(t.dtype) * (h @ w_down[e])
    return y.reshape(b, s, d)

def second_inputs(seed: int = 0) -> dict:
    key = jax.random.key(seed)
    ks = jax.random.split(key, 20)
    f32 = jnp.float32
    d = D_MODEL
    s_in = d ** -0.5
    nrm = lambda k, shape: jax.random.normal(k, shape, f32)
    x = nrm(ks[0], (BATCH, SEQ, d))

    def qkv_cols(k, width):
        kq, kk, kv = jax.random.split(k, 3)
        return [nrm(kq, (DEPTH, d, width)) * s_in,
                nrm(kk, (DEPTH, d, width)) * s_in,
                nrm(kv, (DEPTH, d, width)) * (s_in * BETA)]

    w_in = jnp.concatenate(qkv_cols(ks[1], D_SB) + qkv_cols(ks[2], D_DIL), axis=-1)
    g_sb = 1.0 + 0.05 * nrm(ks[3], (DEPTH, D_SB))
    g_dil = 1.0 + 0.05 * nrm(ks[4], (DEPTH, D_DIL))
    w_out = nrm(ks[5], (DEPTH, d, d)) * (s_in * BETA)
    ln1_g = 1.0 + 0.05 * nrm(ks[6], (DEPTH, d))
    ln1_b = 0.02 * nrm(ks[7], (DEPTH, d))
    ln2_g = 1.0 + 0.05 * nrm(ks[8], (DEPTH, d))
    ln2_b = 0.02 * nrm(ks[9], (DEPTH, d))
    rel_bias = 0.5 * nrm(ks[10], (N_BUCKETS, N_HEADS_DIL))
    w_router = nrm(ks[11], (d, N_EXPERTS_2)) * s_in
    b_router = 0.01 * nrm(ks[12], (N_EXPERTS_2,))
    w_gate = nrm(ks[13], (DEPTH, N_EXPERTS_2, d, D_FF_EXPERT)) * s_in
    w_up = nrm(ks[14], (DEPTH, N_EXPERTS_2, d, D_FF_EXPERT)) * (s_in * BETA)
    w_down = nrm(ks[15], (DEPTH, N_EXPERTS_2, D_FF_EXPERT, d)) * (D_FF_EXPERT ** -0.5 * BETA)
    return {"x": x, "w_in": w_in, "g_sb": g_sb, "g_dil": g_dil, "w_out": w_out,
            "ln1_g": ln1_g, "ln1_b": ln1_b, "ln2_g": ln2_g, "ln2_b": ln2_b,
            "rel_bias": rel_bias, "w_router": w_router, "b_router": b_router,
            "w_gate": w_gate, "w_up": w_up, "w_down": w_down}

def second_block(x, w_in, g_sb, g_dil, w_out, ln1_g, ln1_b, ln2_g, ln2_b,
              rel_bias, w_router, b_router, w_gate, w_up, w_down):
    for l in range(DEPTH):
        h = token_mixer(x, w_in[l], g_sb[l], g_dil[l], w_out[l], rel_bias)
        x = layer_norm_2(ALPHA * x + h, ln1_g[l], ln1_b[l])
        h = grouped_moe(x, w_router, b_router, w_gate[l], w_up[l], w_down[l])
        x = layer_norm_2(ALPHA * x + h, ln2_g[l], ln2_b[l])
    return x


def setup_inputs(seed=0):
    out = dict(first_inputs(seed))
    for name, value in second_inputs(seed + 1).items():
        if name != "x":
            out[name + "_2"] = value
    return out


def reference(
    x, c, ctx, c_ctx, ada_w, ada_b, norm_mix_g, w_in, conv_w, a_log, dt_bias, gdn_norm_g,
    sgu_ln_g, sgu_ln_b, sgu_w, sgu_b, w_branch_a, w_branch_b, w_out, norm_ffn_g, router_group_w,
    router_group_b, router_expert_w, router_expert_b, expert_w1, expert_w3, expert_w2,
    final_norm_g, w_in_2, g_sb_2, g_dil_2, w_out_2, ln1_g_2, ln1_b_2, ln2_g_2, ln2_b_2,
    rel_bias_2, w_router_2, b_router_2, w_gate_2, w_up_2, w_down_2,
):
    x = first_block(
        x, c, ctx, c_ctx, ada_w, ada_b, norm_mix_g, w_in, conv_w, a_log, dt_bias, gdn_norm_g,
        sgu_ln_g, sgu_ln_b, sgu_w, sgu_b, w_branch_a, w_branch_b, w_out, norm_ffn_g,
        router_group_w, router_group_b, router_expert_w, router_expert_b, expert_w1, expert_w3,
        expert_w2, final_norm_g,
    )
    return second_block(
        x, w_in_2, g_sb_2, g_dil_2, w_out_2, ln1_g_2, ln1_b_2, ln2_g_2, ln2_b_2, rel_bias_2,
        w_router_2, b_router_2, w_gate_2, w_up_2, w_down_2,
    )


_drawn_inputs = setup_inputs


def setup_inputs(seed=0):
    import zlib

    import numpy as np

    out = dict(_drawn_inputs(seed))
    spreads = {}
    factors = {'c_ctx': 3.191,
     'sgu_ln_b': 8.0,
     'sgu_b': 2.758,
     'router_group_b': 64.0,
     'router_expert_b': 23.145,
     'ln2_b_2': 2.723,
     'b_router_2': 9.424,
     'gdn_norm_g': 2.837,
     'sgu_ln_g': 2.847}
    for name, (base, spread) in spreads.items():
        noise = np.random.default_rng([zlib.crc32(name.encode()), seed]).standard_normal(out[name].shape)
        drawn = base * np.exp(spread * noise) if base else spread * noise
        out[name] = __import__('jax').numpy.asarray(drawn.astype(out[name].dtype))
    for name, factor in factors.items():
        out[name] = (out[name] * factor).astype(out[name].dtype)
    return out
```

```python
from contextlib import ExitStack

import numpy as np

import concourse.bass as bass
from concourse import mybir

F32 = mybir.dt.float32
ALU = mybir.AluOpType
ACT = mybir.ActivationFunctionType
AX_X = mybir.AxisListType.X

P = 128
D = 1024
KT = D // P
SEQ = 256
TOK = 2 * SEQ
QT = SEQ // P
TT = TOK // P
HEADS = 8
DH = 2 * HEADS
CHUNK = 64
CONV = 5
LEVELS = 6
EPS = 1e-6
LN_EPS = 1e-5
ALPHA = 2.0 ** 0.25
NEG = -1e30
E1, E1_SUB = 32, 1
E2, E2_SUB = 16, 4
GROUPS1, PER1 = 4, 8
GROUPS2, PER2 = 4, 4
FS = 256
H2 = 8
DH2 = 64
BUCKETS = 32
BIAS_W = 2 * SEQ

RING = 3
BLOCKS = 6
GROUP = BLOCKS * D

ADA0 = 0
V0 = ADA0 + 6 * KT
U0 = V0 + KT
Z0 = U0 + KT
G0 = Z0 + KT
AB0 = G0 + 2 * KT
O0 = AB0 + 2 * KT
N_FIRST = O0 + KT
QS0, KS0, VS0, QD0, KD0, VD0, O20 = 0, 4, 8, 12, 16, 20, 24
N_SECOND = O20 + KT
FIRST_GROUPS = -(-N_FIRST // BLOCKS)
SECOND_GROUPS = -(-N_SECOND // BLOCKS)
MOE1_G = FIRST_GROUPS
SECOND_G = MOE1_G + E1 * E1_SUB
MOE2_G = SECOND_G + SECOND_GROUPS
N_GROUPS = MOE2_G + E2 * E2_SUB


def layout(*fields):
    at, out = 0, {}
    for name, n in fields:
        out[name] = slice(at, at + n)
        at += n
    return out, at


ROWS_N = D + GROUPS1 + E1 + E2

VEC, VEC_N = layout(
    ("cond", KT * 2), ("ada_b", 6 * KT), ("norm_mix_g", KT), ("conv_w", 3 * KT * CONV), ("gdn_norm_g", 1),
    ("norm_ffn_g", KT), ("final_norm_g", KT), ("ln1_g", KT), ("ln1_b", KT), ("ln2_g", KT), ("ln2_b", KT),
    ("g_heads", KT), ("dt_bias", DH), ("a_log", DH))
MATS = ["ident", "tri_f", "tri_b", "same"] + [f"level{k}_{d}" for k in range(LEVELS) for d in "fb"]


def shape_constants():
    s, t = np.arange(P)[:, None], np.arange(P)[None, :]
    same = s // CHUNK == t // CHUNK
    mats = {"ident": s == t, "tri_f": same & (s <= t), "tri_b": same & (s >= t), "same": same}
    for k in range(LEVELS):
        b = 1 << k
        up = (s // (2 * b) == t // (2 * b)) & (s // b < t // b)
        mats[f"level{k}_f"], mats[f"level{k}_b"] = up, up.T
    square = np.stack([mats[n] for n in MATS], 1).astype(np.float32)
    q = np.arange(SEQ)
    before = (np.arange(P)[:, None, None] + P * np.arange(QT)[None, :, None]) < q[None, None, :]
    after = s > t
    def count(d):
        return ((d >= 0) & (d <= 128)) * 1 + ((d >= 0) & (d % 4 == 0) & (d <= 512)) + ((d >= 0) & (d % 16 == 0))
    d = (np.arange(P)[:, None, None] + P * np.arange(QT)[None, :, None]) - q[None, None, :]
    attn = np.concatenate([before.reshape(P, -1), count(d).reshape(P, -1), after, s + t == P - 1], 1).astype(np.float32)
    dist = SEQ - 1 - np.arange(BIAS_W)
    half = BUCKETS // 2
    large = half + (np.log(np.maximum(dist, 1).astype(np.float32) / np.float32(half))
                    / np.float32(np.log(2048 / half)) * np.float32(BUCKETS - half)).astype(np.int32)
    bucket = np.where(dist < half, dist, np.minimum(large, BUCKETS - 1))
    bucket = np.where(count(dist) > 0, bucket, BUCKETS)
    onehot = (np.arange(BUCKETS + 1)[:, None] == bucket[None, :]).astype(np.float32)
    return square, attn, onehot


class Chain:

    def __init__(self, engine, sem):
        self.engine, self.sem, self.n, self.step, self.per = engine, sem, 0, None, 0

    def __call__(self, instruction):
        self.n += 1
        instruction.then_inc(self.sem, 1)
        self.engine.wait_ge(self.sem, self.n if self.step is None else self.start + self.step * self.per + self.n)

    def enter(self, step, per):
        self.start, self.step, self.per, self.n = self.n, step, per, 0

    def leave(self, turns):
        assert self.n == self.per, (self.n, self.per)
        self.n, self.step = self.start + turns * self.per, None


def chunk_of(n, d):
    per = SEQ // CHUNK
    seq, i = divmod(n, per)
    c = seq * per + (i if d == 0 else per - 1 - i)
    return c // 2, (c % 2) * CHUNK


def build(nc, t):
    ctx = ExitStack()
    with ctx:
        def sb(name, *shape):
            return ctx.enter_context(nc.sbuf_tensor(name, [P, *shape], F32))

        def sem(name):
            return ctx.enter_context(nc.semaphore(name))

        ring = sb("ring", RING, GROUP)
        head_w = sb("head_w", 3, KT, P)
        xc = sb("xc", KT, TOK)
        hc = sb("hc", KT, TOK)
        o_heads = sb("o_heads", HEADS, SEQ)
        mats = sb("mats", len(MATS), P)
        ones = sb("ones", P)
        vec = sb("vec", VEC_N)
        ba_w = sb("ba_w", KT, 2 * DH)
        arena = sb("arena", 33 * 512)
        cs = sb("cs", KT, 2)
        mod = sb("mod", 6 * KT, 2)
        mixs = sb("mixs", KT, 2)
        ffns = sb("ffns", KT)
        gates_in = sb("gates_in", TT, 2 * DH)
        gd = {n: sb(f"gd_{n}", TT, DH) for n in ("beta", "g", "G", "kb", "kd", "t")}
        bank = [ctx.enter_context(nc.psum_tensor(f"bank{i}", [P, 512], F32)) for i in range(8)]
        bias_dram = nc.dram_tensor("bias_rows", (H2, BIAS_W), F32, kind="Internal").ap()

        X, H = xc[:, :, SEQ:TOK], hc[:, :, SEQ:TOK]
        XS, HS = xc[:, :, 0:SEQ], hc[:, :, 0:SEQ]

        def M(name):
            return mats[:, MATS.index(name), :]

        def V(name):
            return vec[:, VEC[name]]

        def area(at, *shape):
            n = int(np.prod(shape))
            a = arena[:, at:at + n]
            if len(shape) == 2:
                return a.rearrange("p (a b) -> p a b", a=shape[0])
            if len(shape) == 3:
                return a.rearrange("p (a b c) -> p a b c", a=shape[0], b=shape[1])
            return a

        def over(ap, n):
            return ap.unsqueeze(len(ap.shape)).broadcast_to([*ap.shape, n])

        def times(ap, n):
            return ap.unsqueeze(1).broadcast_to([ap.shape[0], n, *ap.shape[1:]])

        def place(i):
            return area(512 * i, TT, P)
        conv = [place(0), place(1), place(2)]
        tmp = [place(3), place(4)]
        rhs = [place(5), place(6), place(7), place(8)]
        levels = rhs
        vb, kb, kd = [place(9), place(10)], [place(11), place(12)], [place(13), place(14)]
        et, qd, qk = [place(15), place(16)], [place(17), place(18)], [place(19), place(20)]
        up = [place(21), place(22)]
        E_, D_, Y_ = [place(23), place(24)], [place(25), place(26)], [place(27), place(28)]
        pad = [area(512 * 29 + 520 * j, 2, SEQ + 4) for j in range(3)]
        state = [area(512 * 29 + 1560 + P * d, P) for d in range(2)]
        u_, w_ = D_, Y_

        v_rows, u_cols, z_cols = area(0, QT, D), area(2048, KT, SEQ), area(4096, KT, SEQ)
        gate_cols = area(6144, KT, 2 * SEQ)
        y_gdn, y_sgu, merged = area(10240, KT, SEQ), area(12288, KT, SEQ), area(14336, KT, SEQ)
        r_gdn = area(12288, 4, 512)
        sq_gdn = area(14336, 4, 512)
        hw = head_w[:, :, :, :].rearrange("p a k n -> p (a k n)")
        ln_rows = hw[:, 0:2 * D].rearrange("p (a n) -> p a n", a=2)
        sgu_wT = hw[:, 2 * D:3 * D].rearrange("p (g n) -> p g n", g=KT)
        bn = sb("bn", QT, 2, 6)
        bn_mv = sb("bn_mv", QT, 2)
        bn_r = sb("bn_r", QT)
        one_row = sb("one_row", 1, ROWS_N)
        eps = sb("eps", 3)
        eps_ap = {EPS: eps[:, 0:1], LN_EPS: eps[:, 1:2], 1.0: eps[:, 2:3]}

        gate_bc = area(0, E1, SEQ)
        silu_h = [area(8192 + 512 * i, 512) for i in range(2)]
        hid = [area(9216 + 512 * i, 2, SEQ) for i in range(2)]
        norm_r = area(10240, SEQ)
        norm_m = area(10496, SEQ)
        router_w = [area(10752, KT, GROUPS1 + E1), area(10752 + KT * (GROUPS1 + E1), KT, E2)]
        rt = [area(11264 + 64 * i, 2 * 32) for i in range(10)]
        rs = [area(12032 + 16 * i, 16) for i in range(10)]
        gate_rows = area(12288, QT, E1)
        gate_T = area(12416, SEQ)

        qs, ks, vs = area(0, 4, SEQ), area(1024, 4, SEQ), area(2048, QT, 512)
        qd2, kd2, vd2 = area(3072, 4, SEQ), area(4096, 4, SEQ), area(5120, QT, 512)
        o_att = area(6144, KT, SEQ)
        bias2 = area(8192, H2, QT, SEQ)
        sc = [area(12288 + 512 * i, QT, SEQ) for i in range(6)]
        sq_att = area(0, 4, 512)
        r_att = area(2048, 4, 512)
        am = sb("am", 4, QT)
        attn_c = hw
        before = attn_c[:, 0:512].rearrange("p (a n) -> p a n", a=QT)
        count = attn_c[:, 512:1024].rearrange("p (a n) -> p a n", a=QT)
        after = attn_c[:, 1024:1024 + P]
        flip = attn_c[:, 1024 + P:1024 + 2 * P]
        rel = o_heads[0:BUCKETS + 1, 0, 0:H2]
        onehot = o_heads[0:BUCKETS + 1, 1:3, :].rearrange("p a n -> p (a n)")
        bias_row = o_heads[0:H2, 3:5, :].rearrange("p a n -> p (a n)")

        S = {}

        class Sems:
            def __getitem__(self, name):
                if name not in S:
                    S[name] = sem(name)
                return S[name]
        s = Sems()
        landed = [sem(f"slot{i}_landed") for i in range(RING)]
        slots_used = sem("slots_used")

        def group_view(g):
            return ring[:, g % RING, :]

        def block_view(first_group, j):
            g = first_group + j // BLOCKS
            at = (j % BLOCKS) * D
            return ring[:, g % RING, at:at + D].rearrange("p (k n) -> p k n", k=KT)

        block = ctx.enter_context(nc.Block())

        @block.sync
        def _(sp):
            sp.dma_start(vec[:, :], t["vec"]).then_inc(s["vec_landed"], 16)
            sp.dma_start(xc[:, :, :], t["xc"]).then_inc(s["xc_landed"], 16)
            sp.dma_start(mats[:, :, :], t["square"]).then_inc(s["mats_landed"], 16)
            for g in range(RING):
                sp.dma_start(ring[:, g, :], t["stream"][g]).then_inc(landed[g], 16)
            turns = (N_GROUPS - RING) // RING
            with sp.Fori(0, turns) as i:
                for k in range(RING):
                    sp.wait_ge(slots_used, RING * i + (k + 1))
                    sp.dma_start(ring[:, k, :], t["stream"][bass.ds(RING * i + (RING + k), 1)].rearrange("a p n -> (a p) n")
                                 ).then_inc(landed[k], 16)
            for g in range(RING * (turns + 1), N_GROUPS):
                sp.wait_ge(slots_used, g - RING + 1)
                sp.dma_start(ring[:, g % RING, :], t["stream"][g]).then_inc(landed[g % RING], 16)
            sp.wait_ge(s["ln2_done"], 1)
            sp.dma_start(t["out"], X).then_inc(s["stored"], 16)
            sp.wait_ge(s["stored"], 16)

        @block.gpsimd
        def _(pool):
            nc.gpsimd.memset(o_heads[BUCKETS:BUCKETS + 1, 0, 0:H2], NEG).then_inc(s["rel_set"], 1)
            pool.dma_start(o_heads[0:BUCKETS, 0, 0:H2], t["rel_bias"]).then_inc(s["rel_landed"], 16)
            pool.dma_start(onehot, t["onehot"]).then_inc(s["rel_landed"], 16)
            pool.dma_start(ba_w[:, :, :], t["ba_w"]).then_inc(s["ba_landed"], 16)
            pool.dma_start(one_row[0:1, 0, :], t["rows"]).then_inc(s["rows_landed"], 16)
            pool.dma_start(hw, t["head_w"][0]).then_inc(s["head_landed"], 16)
            pool.wait_ge(s["bias_copied"], 1)
            pool.dma_start(bias_dram, bias_row).then_inc(s["bias_stored"], 16)
            link = Chain(pool, s["pool_chain"])
            pool.wait_ge(s["g_ready"], 1)
            pool.wait_ge(s["mats_landed"], 16)
            pool.wait_ge(s["bias_stored"], 16)
            with pool.Fori(0, HEADS) as h:
                pool.wait_ge(s["head_free"], h + 1)
                for d in range(2):
                    col = bass.ds(h + HEADS * d, 1)
                    tri = M("tri_f" if d == 0 else "tri_b")
                    nc.gpsimd.tensor_tensor(rhs[d], times(tri, TT), gd["g"][:, :, col].broadcast_to([P, TT, P]),
                                            ALU.mult).then_inc(s["rhs_ready"], 1)
                for d in range(2):
                    col = bass.ds(h + HEADS * d, 1)
                    nc.gpsimd.tensor_tensor(rhs[2 + d], times(M("ident"), TT),
                                            gd["beta"][:, :, col].broadcast_to([P, TT, P]),
                                            ALU.mult).then_inc(s["rhs_ready"], 1)
                for d in range(2):
                    pool.wait_ge(s["decays"], 2 * h + (d + 1))
                    nc.gpsimd.tensor_tensor(et[d], et[d], times(M("tri_f" if d == 0 else "tri_b"), TT),
                                            ALU.mult).then_inc(s["masked"], 1)
                for d in range(2):
                    pool.wait_ge(s["exp_g"], 2 * h + (d + 1))
                    pool.wait_ge(s["normed"], 2 * h + 2)
                    nc.gpsimd.tensor_tensor(qd[d], conv[0], tmp[d], ALU.mult).then_inc(s["q_decayed"], 1)
                pool.wait_ge(s["gram"], 8 * h + 8)
                for k in range(LEVELS):
                    for d in range(2):
                        if k == 0:
                            pool.wait_ge(s["couplings"], 2 * h + (d + 1))
                        elif k == 2:
                            pool.wait_ge(s["first_inverse"], 2 * h + (d + 1))
                        elif k > 2:
                            pool.wait_ge(s["y_made"], 10 * h + (2 * (k - 3) + d + 1))
                        nc.gpsimd.tensor_tensor(levels[2 * (k % 2) + d], up[d], times(M(f"level{k}_{'fb'[d]}"), TT),
                                                ALU.mult).then_inc(s["level_masked"], 1)
                pool.wait_ge(s["projected"], 3 * h + 3)
                pool.dma_start(hw,
                               t["head_w"][bass.ds(h + 1, 1)].rearrange("a p n -> (a p) n")
                               ).then_inc(s["head_landed"], 16)
            pool.wait_ge(s["residual1"], KT)
            pool.dma_start(arena[:, 10752:10752 + KT * (GROUPS1 + E1 + E2)], t["router_w"]).then_inc(s["router_landed"], 16)
            pool.dma_start(hw[:, 0:1024 + 2 * P], t["attn"]).then_inc(s["attn_landed"], 16)
            pool.wait_ge(s["x3_ready"], 1)
            for qt in range(QT):
                rows = bass.AP(tensor=bias_dram.tensor, offset=SEQ - P - qt * P, ap=[[1, P], [BIAS_W, H2], [1, SEQ]])
                pool.dma_start(bias2[:, :, qt, :], rows).then_inc(s["bias_landed"], 16)
            pool.wait_ge(s["bias_landed"], 32)
            pool.wait_ge(s["residual3"], KT)
            pool.dma_start(arena[:, 10752:10752 + KT * (GROUPS1 + E1 + E2)], t["router_w"]).then_inc(s["router_landed"], 16)

        @block.tensor
        def _(pe):
            def mm(out, lhsT, rhs_, start=True, stop=True, **kw):
                return nc.tensor.matmul(out, lhsT, rhs_, start=start, stop=stop, **kw)

            group_ended = False

            def release(ins):
                nonlocal group_ended
                if group_ended:
                    ins.then_inc(slots_used, 1)
                group_ended = False

            def block_of(first_group, j, last):
                g = first_group + j // BLOCKS
                if j % BLOCKS == 0:
                    pe.wait_ge(landed[g % RING], 16 * (g // RING + 1))
                return block_view(first_group, j)

            def block_ends(j, last):
                nonlocal group_ended
                group_ended = j % BLOCKS == BLOCKS - 1 or j == last

            def project(bank_ap, w, moving, ks=KT, **kw):
                for k in range(ks):
                    ins = mm(bank_ap, w[:, k, :], moving[:, k, :], k == 0, k == ks - 1, **kw)
                    if k == 0:
                        release(ins)
                return ins

            def project_rows(acc, w, src, first):
                for qt in range(QT):
                    for k in range(KT):
                        at = first + qt * P
                        ins = mm(acc[:, qt * P:(qt + 1) * P], src[:, k, at:at + P], w[:, k, :], k == 0, k == KT - 1)
                        if k == 0:
                            release(ins)
                return ins

            def column_sum(out, src, n=KT):
                for k in range(n):
                    ins = mm(out, ones[:, :], src[:, k, :], k == 0, k == n - 1)
                    if k == 0:
                        release(ins)
                return ins

            pe.wait_ge(s["ones_set"], 1)
            pe.wait_ge(s["rel_landed"], 32)
            pe.wait_ge(s["rel_set"], 1)
            mm(bank[0][0:H2, :], rel, onehot).then_inc(s["bias_made"], 1)
            pe.wait_ge(s["xc_squared"], 1)
            column_sum(bank[1][:, :], hc).then_inc(s["xc_summed"], 1)
            pe.wait_ge(s["cond_ready"], 1)
            for j in range(6 * KT):
                w = block_of(0, j, N_FIRST - 1)
                ins = project(bank[2][:, 2 * j:2 * j + 2], w, cs)
                block_ends(j, N_FIRST - 1)
            ins.then_inc(s["mod_made"], 1)
            pe.wait_ge(s["modulated"], KT)
            pe.wait_ge(s["ba_landed"], 16)
            for tt in range(TT):
                for k in range(KT):
                    ins = mm(bank[0][:, tt * 2 * DH:(tt + 1) * 2 * DH], hc[:, k, tt * P:(tt + 1) * P], ba_w[:, k, :],
                             k == 0, k == KT - 1)
                    release(ins)
            ins.then_inc(s["ba_made"], 1)
            pe.wait_ge(s["g_raw"], 1)
            pe.wait_ge(s["mats_landed"], 16)
            g = gd["g"]
            mm(bank[1][:, 0:32].rearrange("p (a b) -> p a b", a=TT), M("tri_f"), g[:, :, 0:HEADS])
            mm(bank[1][:, 32:64].rearrange("p (a b) -> p a b", a=TT), M("tri_b"), g[:, :, HEADS:DH])
            mm(bank[1][:, 64:128], M("same"), g[:, :, :].rearrange("p a b -> p (a b)")).then_inc(s["cum_made"], 1)

            with pe.Fori(0, HEADS) as h:
                pe.wait_ge(s["head_free"], h + 1)
                pe.wait_ge(s["head_landed"], 16 * h + 16)
                for j in range(3):
                    project(bank[j][:, :], head_w[:, j, :, :], hc).then_inc(s["projected"], 1)
                for j in range(2):
                    pe.wait_ge(s["squared"], 2 * h + (j + 1))
                    mm(bank[3 + j][:, :], ones[:, :], tmp[j].rearrange("p a b -> p (a b)")).then_inc(s["sq_summed"], 1)
                pe.wait_ge(s["rhs_ready"], 4 * h + 4)
                pe.wait_ge(s["padded"], 3 * h + 3)
                for d in range(2):
                    mm(bank[1 + d][:, :], ones[:, :], rhs[d].rearrange("p a b -> p (a b)")).then_inc(s["gram"], 1)
                pe.wait_ge(s["norms_ready"], 2 * h + 2)
                for d in range(2):
                    mm(bank[3 + d][:, :], ones[:, :], rhs[2 + d].rearrange("p a b -> p (a b)")).then_inc(s["gram"], 1)
                pe.wait_ge(s["normed"], 2 * h + 1)
                for a in range(TT):
                    ins = nc.tensor.transpose(bank[5][:, a * P:(a + 1) * P], conv[1][:, a, :], M("ident"))
                ins.then_inc(s["gram"], 1)
                pe.wait_ge(s["activated"], 3 * h + 3)
                for a in range(TT):
                    ins = nc.tensor.transpose(bank[6][:, a * P:(a + 1) * P], conv[2][:, a, :], M("ident"))
                ins.then_inc(s["gram"], 1)
                for a in range(TT):
                    ins = mm(bank[7][:, a * P:(a + 1) * P], conv[1][:, a, :], conv[1][:, a, :])
                ins.then_inc(s["gram"], 1)
                pe.wait_ge(s["normed"], 2 * h + 2)
                for a in range(TT):
                    ins = mm(bank[0][:, a * P:(a + 1) * P], conv[1][:, a, :], conv[0][:, a, :])
                ins.then_inc(s["gram"], 1)
                for d in range(2):
                    pe.wait_ge(s["first_inverse"], 2 * h + (d + 1))
                    pe.wait_ge(s["exp_g"], 2 * h + 2)
                    for a in range(TT):
                        ins = nc.tensor.transpose(bank[1 + d][:, a * P:(a + 1) * P], E_[d][:, a, :], M("ident"))
                    ins.then_inc(s["inverse_turned"], 1)
                for k in range(1, LEVELS):
                    for d in range(2):
                        pe.wait_ge(s["level_masked"], 12 * h + (2 * k + d + 1))
                        if k == 1:
                            pe.wait_ge(s["d_copied"], 2 * h + (d + 1))
                        else:
                            pe.wait_ge(s["d_updated"], 8 * h + (2 * (k - 2) + d + 1))
                            pe.wait_ge(s["y_copied"], 10 * h + (2 * (k - 2) + d + 1))
                        for a in range(TT):
                            ins = mm(bank[3 + d][:, a * P:(a + 1) * P], levels[2 * (k % 2) + d][:, a, :], D_[d][:, a, :])
                        ins.then_inc(s["y_made"], 1)
                    for d in range(2):
                        pe.wait_ge(s["y_copied"], 10 * h + (2 * (k - 1) + d + 1))
                        if k > 1:
                            pe.wait_ge(s["e_updated"], 10 * h + (2 * (k - 2) + d + 1))
                        if k < LEVELS - 1:
                            for a in range(TT):
                                ins = mm(bank[5 + d][:, a * P:(a + 1) * P], E_[d][:, a, :], Y_[d][:, a, :])
                            ins.then_inc(s["dy_made"], 1)
                        for a in range(TT):
                            ins = mm(bank[1 + d][:, a * P:(a + 1) * P], Y_[d][:, a, :], E_[d][:, a, :])
                        ins.then_inc(s["ey_made"], 1)
                for d in range(2):
                    pe.wait_ge(s["e_updated"], 10 * h + (2 * (LEVELS - 2) + d + 1))
                    for a in range(TT):
                        ins = mm(bank[3 + d][:, a * P:(a + 1) * P], E_[d][:, a, :], vb[d][:, a, :])
                    ins.then_inc(s["uw_made"], 1)
                for d in range(2):
                    for a in range(TT):
                        ins = mm(bank[5 + d][:, a * P:(a + 1) * P], kb[d][:, a, :], E_[d][:, a, :])
                    ins.then_inc(s["uw_made"], 1)
                n_chunks = TOK // CHUNK
                for n in range(n_chunks):
                    for d in range(2):
                        c, r = chunk_of(n, d)
                        half = slice(r, r + CHUNK)
                        if n == 0:
                            pe.wait_ge(s["uw_copied"], 4 * h + 4)
                            pe.wait_ge(s["q_decayed"], 2 * h + 2)
                            pe.wait_ge(s["rows_scaled"], 6 * h + 6)
                        else:
                            pe.wait_ge(s["stepped"], 14 * h + (2 * (n - 1) + d + 1))
                            mm(bank[(0, 7)[d]][half, 0:P], w_[d][:, c, half], state[d]).then_inc(s["ws_made"], 1)
                    for d in range(2):
                        c, r = chunk_of(n, d)
                        half = slice(r, r + CHUNK)
                        if n > 0:
                            pe.wait_ge(s["v_new"], 14 * h + (2 * (n - 1) + d + 1))
                        if n >= n_chunks // 2:
                            at = (2 * (c - QT) * CHUNK) + r
                            out = bank[3 + d][:, at:at + CHUNK]
                            mm(out, state[d], qd[d][:, c, half], True, False)
                            ins = mm(out, u_[d][half, c, :], qk[d][half, c, half], False, True)
                            if n == n_chunks - 1:
                                ins.then_inc(s["o_made"], 1)
                        if n < n_chunks - 1:
                            mm(bank[1 + d][:, 0:P], kd[d][half, c, :], u_[d][half, c, :]).then_inc(s["kv_made"], 1)

            pe.wait_ge(s["head_free"], HEADS + 1)
            pe.wait_ge(s["o_squared"], 1)
            for i in range(4):
                mm(bank[4 + i][:, :], ones[:, :], sq_gdn[:, i, :]).then_inc(s["o_summed"], 1)
            n = 0

            def acc_bank():
                nonlocal n
                if n >= 4:
                    pe.wait_ge(s["rest_taken"], n - 3)
                n += 1
                return bank[(n - 1) % 4]

            for j in range(KT):
                acc = acc_bank()
                w = block_of(0, V0 + j, N_FIRST - 1)
                project_rows(acc, w, hc, SEQ).then_inc(s["rest_made"], 1)
                block_ends(V0 + j, N_FIRST - 1)
            for first in (U0, Z0):
                for j in range(KT):
                    acc = acc_bank()
                    w = block_of(0, first + j, N_FIRST - 1)
                    project(acc[:, 0:SEQ], w, H).then_inc(s["rest_made"], 1)
                    block_ends(first + j, N_FIRST - 1)

            def pair(first, j, moving):
                acc = acc_bank()
                for i in range(2):
                    w = block_of(0, first + 2 * j + i, N_FIRST - 1)
                    ins = project(acc[:, i * SEQ:(i + 1) * SEQ], w, moving[i])
                    block_ends(first + 2 * j + i, N_FIRST - 1)
                ins.then_inc(s["rest_made"], 1)

            for j in range(KT):
                pair(G0, j, (H, H))
            pe.wait_ge(s["v_normed"], 1)
            pe.wait_ge(s["head_landed"], 16 * (HEADS + 1))
            pe.wait_ge(s["rows_landed"], 16)
            for j in range(KT):
                if j >= 3:
                    pe.wait_ge(s["sgu_taken"], j - 2)
                for qt in range(QT):
                    out = bank[4 + j % 3][:, qt * P:(qt + 1) * P]
                    mm(out, v_rows[:, qt, j * P:(j + 1) * P], sgu_wT[:, j, :], True, False)
                    ins = mm(out, ones[0:1, :], one_row[0:1, 0, j * P:(j + 1) * P], False, True)
                ins.then_inc(s["sgu_mixed"], 1)
            pe.wait_ge(s["sgu_taken"], KT)
            for j in range(KT):
                pair(AB0, j, (y_gdn, y_sgu))
            pe.wait_ge(s["rest_taken"], n)
            for j in range(KT):
                if j >= 4:
                    pe.wait_ge(s["residual1"], j - 3)
                w = block_of(0, O0 + j, N_FIRST - 1)
                project(bank[j % 4][:, 0:SEQ], w, merged).then_inc(s["rest_made"], 1)
                block_ends(O0 + j, N_FIRST - 1)

            def norm_sum(name):
                pe.wait_ge(s[name + "_ready"], 1)
                column_sum(bank[4][:, 0:SEQ], HS).then_inc(s[name + "_summed"], 1)

            def route(m, width, experts):
                pe.wait_ge(s[f"route_in{m}"], KT if m == 0 else 1)
                pe.wait_ge(s["router_landed"], 16 * (m + 1))
                src = H if m == 0 else X
                for qt in range(QT):
                    out = bank[5][:, qt * width:(qt + 1) * width]
                    for k in range(KT):
                        mm(out, src[:, k, qt * P:(qt + 1) * P], router_w[m][:, k, :], k == 0, False)
                    at = D + (0, GROUPS1 + E1)[m]
                    ins = mm(out, ones[0:1, :], one_row[0:1, 0, at:at + width], False, True)
                ins.then_inc(s["logits_made"], 1)
                pe.wait_ge(s["gates_ready"], m + 1)
                for qt in range(QT):
                    ins = nc.tensor.transpose(bank[6][0:experts, qt * P:(qt + 1) * P], gate_rows[:, qt, 0:experts], M("ident"))
                ins.then_inc(s["gates_turned"], 1)
                pe.wait_ge(s["gates_turned_copied"], m + 1)
                done = (0, E1 // 2)[m]
                for e in range(0, experts, 2):
                    i = done + e // 2
                    if e >= 8:
                        pe.wait_ge(s["gates_spread_copied"], i - 3)
                    for k in range(2):
                        pick = mats[0:experts, 0, e + k:e + k + 1].broadcast_to([experts, P])
                        ins = mm(bank[(e // 2) % 4][:, k * SEQ:(k + 1) * SEQ], pick, gate_T[0:experts, :])
                    ins.then_inc(s["gates_spread"], 1)
                pe.wait_ge(s["gates_spread_copied"], done + experts // 2)

            def mixture(m, group0, slices, src):
                def expert_up(slot, b, step_landed):
                    pe.wait_ge(landed[slot], step_landed)
                    w = ring[:, slot, :]
                    for w0, acc in ((0, bank[2 * b]), (KT * FS, bank[2 * b + 1])):
                        wv = w[:, w0:w0 + KT * FS].rearrange("p (k f) -> p k f", k=KT)
                        for f in range(2):
                            for k in range(KT):
                                ins = mm(acc[:, f * SEQ:(f + 1) * SEQ], wv[:, k, f * P:(f + 1) * P], src[:, k, :],
                                         k == 0, k == KT - 1)
                    ins.then_inc(s[f"up_made{m}"], 1)

                def expert_down(slot, b, hid_count, stop):
                    pe.wait_ge(s[f"hid_ready{m}"], hid_count)
                    w = ring[:, slot, 2 * KT * FS:].rearrange("p (f d) -> p f d", f=2)
                    for j in range(KT):
                        for f in range(2):
                            ins = mm(bank[4 + j // 2][:, (j % 2) * SEQ:(j % 2 + 1) * SEQ], w[:, f, j * P:(j + 1) * P],
                                     hid[b][:, f, :], False, stop and f == 1, skip_group_check=True)
                    ins.then_inc(slots_used, 1)

                def need(e):
                    return 16 * ((group0 + e) // RING + 1)

                pe.wait_ge(s[f"acc_zeroed{m}"], 1)
                expert_up(group0 % RING, 0, need(0))
                turns = (slices - 1) // 6
                with pe.Fori(0, turns) as i:
                    for k in range(6):
                        expert_up((group0 + k + 1) % RING, (k + 1) % 2, 32 * i + need(k + 1))
                        expert_down((group0 + k) % RING, k % 2, 6 * i + (k + 1), False)
                for e in range(6 * turns, slices):
                    if e + 1 < slices:
                        expert_up((group0 + e + 1) % RING, (e + 1) % 2, need(e + 1))
                    expert_down((group0 + e) % RING, e % 2, e + 1, e == slices - 1)

            norm_sum("ffn")
            route(0, GROUPS1 + E1, E1)
            mixture(0, MOE1_G, E1 * E1_SUB, H)
            norm_sum("final")

            pe.wait_ge(s["x3_ready"], 1)
            n2 = 0
            for j in range(O20):
                if n2 >= 4:
                    pe.wait_ge(s["qkv2_taken"], n2 - 3)
                acc = bank[n2 % 4]
                n2 += 1
                w = block_of(SECOND_G, j, N_SECOND - 1)
                if VS0 <= j < QD0 or j >= VD0:
                    ins = project_rows(acc, w, X, 0)
                else:
                    ins = project(acc[:, 0:SEQ], w, X)
                ins.then_inc(s["qkv2_made"], 1)
                block_ends(j, N_SECOND - 1)
            pe.wait_ge(s["qkv2_taken"], O20)
            pe.wait_ge(s["attn_landed"], 16)
            def sb_scores(a):
                rows = slice(DH2 * (a % 2), DH2 * (a % 2) + DH2)
                if a >= 2:
                    pe.wait_ge(s["sb_exponent"], a - 1)
                for kt in range(QT):
                    ins = mm(bank[a % 2][:, kt * SEQ:(kt + 1) * SEQ], ks[rows, a // 2, kt * P:(kt + 1) * P], qs[rows, a // 2, :])
                ins.then_inc(s["sb_scored"], 1)

            def sb_between(a):
                pe.wait_ge(s["sb_logs"], a + 1)
                lm = sc[2 + a % 2]
                out = bank[2 + a % 2]
                mm(out[:, SEQ:2 * SEQ], after, lm[:, 1, :])
                mm(out[:, 0:SEQ], after, lm[:, 0, :], True, False)
                mm(out[:, 0:SEQ], ones[:, :], lm[:, 1, :], False, True).then_inc(s["sb_between"], 1)

            def sb_values(a):
                rows = slice(DH2 * (a % 2), DH2 * (a % 2) + DH2)
                pe.wait_ge(s["sb_weights"], a + 1)
                if a >= 4:
                    pe.wait_ge(s["sb_o_taken"], a // 2 - 1)
                for kt in range(QT):
                    ins = mm(bank[4 + (a // 2) % 2][rows, 0:SEQ], vs[:, kt, a * DH2:(a + 1) * DH2], sc[4 + a % 2][:, kt, :],
                             kt == 0, kt == QT - 1)
                ins.then_inc(s["sb_valued"], 1)

            for a in range(H2 + 2):
                if a < H2:
                    sb_scores(a)
                if 1 <= a <= H2:
                    sb_between(a - 1)
                if a >= 2:
                    sb_values(a - 2)

            pe.wait_ge(s["sb_o_taken"], H2 // 2)
            pe.wait_ge(s["bias_landed"], 32)

            def dl_scores(a):
                rows = slice(DH2 * (a % 2), DH2 * (a % 2) + DH2)
                if a >= 2:
                    pe.wait_ge(s["dl_exped"], 2 * (a - 1))
                for qt in range(QT):
                    out = bank[a % 2][:, qt * SEQ:(qt + 1) * SEQ]
                    mm(out, qd2[rows, a // 2, qt * P:(qt + 1) * P], kd2[rows, a // 2, :], True, False)
                    ins = mm(out, flip, bias2[:, a, qt, :], False, True)
                ins.then_inc(s["dl_scored"], 1)

            def dl_turn(a):
                pe.wait_ge(s["dl_probs"], a + 1)
                if a >= 2:
                    pe.wait_ge(s["dl_turned_copied"], a - 1)
                for kt in range(QT):
                    for qt in range(QT):
                        ins = nc.tensor.transpose(bank[2 + a % 2][:, kt * SEQ + qt * P:kt * SEQ + (qt + 1) * P],
                                                  sc[2 + a % 2][:, qt, kt * P:(kt + 1) * P], M("ident"))
                ins.then_inc(s["dl_turned"], 1)

            def dl_values(a):
                rows = slice(DH2 * (a % 2), DH2 * (a % 2) + DH2)
                pe.wait_ge(s["dl_turned_copied"], a + 1)
                if a >= 4:
                    pe.wait_ge(s["dl_o_taken"], a // 2 - 1)
                for kt in range(QT):
                    ins = mm(bank[4 + (a // 2) % 2][rows, 0:SEQ], vd2[:, kt, a * DH2:(a + 1) * DH2], sc[4 + a % 2][:, kt, :],
                             kt == 0, kt == QT - 1)
                ins.then_inc(s["dl_valued"], 1)

            for a in range(H2 + 2):
                if a < H2:
                    dl_scores(a)
                if 1 <= a <= H2:
                    dl_turn(a - 1)
                if a >= 2:
                    dl_values(a - 2)
            pe.wait_ge(s["att_squared"], 1)
            for i in range(4):
                mm(bank[i][:, :], M("same"), sq_att[:, i, :]).then_inc(s["att_summed"], 1)
            pe.wait_ge(s["att_normed"], 1)
            for j in range(KT):
                if j >= 4:
                    pe.wait_ge(s["residual3"], j - 3)
                w = block_of(SECOND_G, O20 + j, N_SECOND - 1)
                project(bank[j % 4][:, 0:SEQ], w, o_att).then_inc(s["out2_made"], 1)
                block_ends(O20 + j, N_SECOND - 1)

            def layer_norm_sums(name, before_it):
                pe.wait_ge(s[before_it], KT)
                column_sum(bank[4][:, 0:SEQ], X).then_inc(s[name + "_mean"], 1)
                pe.wait_ge(s[name + "_sq"], 1)
                column_sum(bank[5][:, 0:SEQ], HS).then_inc(s[name + "_var"], 1)

            layer_norm_sums("ln1", "residual3")
            route(1, E2, E2)
            mixture(1, MOE2_G, E2 * E2_SUB, X)
            layer_norm_sums("ln2", "residual4")

        @block.scalar
        def _(act):
            link = Chain(act, s["act_chain"])

            def act_fn(out, in_, func, **kw):
                return nc.scalar.activation(out, in_, func, **kw)

            act.wait_ge(s["vec_landed"], 16)
            act_fn(cs[:, :, :].rearrange("p a b -> p (a b)"), V("cond"), ACT.Silu).then_inc(s["cond_ready"], 1)
            act.wait_ge(s["bias_made"], 1)
            act_fn(bias_row, bank[0][0:H2, :], ACT.Copy).then_inc(s["bias_copied"], 1)
            act.wait_ge(s["xc_landed"], 16)
            act_fn(hc[:, :, :], xc[:, :, :], ACT.Square).then_inc(s["xc_squared"], 1)

            def rsqrt(out, in_, scale, eps):
                link(act_fn(out, in_, ACT.Ln, scale=scale, bias=eps_ap[eps]))
                return act_fn(out, out, ACT.Exp, scale=-0.5)

            act.wait_ge(s["xc_summed"], 1)
            act.wait_ge(s["eps_set"], 3)
            rsqrt(area(0, 512), bank[1][:, :], 1.0 / D, EPS).then_inc(s["xc_rnorm"], 1)
            act.wait_ge(s["a_in"], 1)
            act_fn(gd["beta"][:, :, :], gates_in[:, :, 0:DH], ACT.Sigmoid).then_inc(s["beta_ready"], 1)
            link(act_fn(gd["t"][:, :, :], gates_in[:, :, DH:2 * DH], ACT.Abs))
            link(act_fn(gd["t"][:, :, :], gd["t"][:, :, :], ACT.Exp, scale=-1.0))
            act_fn(gd["t"][:, :, :], gd["t"][:, :, :], ACT.Ln, bias=eps_ap[1.0]).then_inc(s["soft_ready"], 1)
            act_fn(gd["kb"][:, 0, :], V("a_log"), ACT.Exp).then_inc(s["soft_ready"], 1)
            act.wait_ge(s["cum_ready"], 1)
            act_fn(gd["t"][:, :, :], gd["G"][:, :, :], ACT.Exp).then_inc(s["cum_exp"], 1)
            act_fn(gd["kd"][:, :, :], gd["kd"][:, :, :], ACT.Exp).then_inc(s["cum_exp"], 1)

            act.wait_ge(s["pads_zeroed"], 3)
            with act.Fori(0, HEADS) as h:
                link.enter(h, 2)
                for j in range(3):
                    act.wait_ge(s["projected"], 3 * h + (j + 1))
                    act_fn(pad[j][:, :, 2:2 + SEQ], bank[j][:, :].rearrange("p (a b) -> p a b", a=2), ACT.Copy
                           ).then_inc(s["padded"], 1)
                for j in range(3):
                    act.wait_ge(s["conved"], 3 * h + (j + 1))
                    act_fn(conv[j], conv[j], ACT.Silu).then_inc(s["activated"], 1)
                for j in range(2):
                    act.wait_ge(s["activated"], 3 * h + (j + 1))
                    act_fn(tmp[j], conv[j], ACT.Square).then_inc(s["squared"], 1)
                for j in range(2):
                    act.wait_ge(s["sq_summed"], 2 * h + (j + 1))
                    r = tmp[j].rearrange("p a b -> p (a b)")
                    rsqrt(r, bank[3 + j][:, :], 1.0, EPS).then_inc(s["norms_ready"], 1)
                for d in range(2):
                    act.wait_ge(s["g_diffs"], 2 * h + (d + 1))
                    act_fn(et[d], et[d], ACT.Exp).then_inc(s["decays"], 1)
                act.wait_ge(s["normed"], 2 * h + 2)
                for d in range(2):
                    act_fn(tmp[d].rearrange("p a b -> p (a b)"), bank[1 + d][:, :], ACT.Exp).then_inc(s["exp_g"], 1)
                for d in range(2):
                    act.wait_ge(s["inverse_turned"], 2 * h + (d + 1))
                    act_fn(D_[d].rearrange("p a b -> p (a b)"), bank[1 + d][:, :], ACT.Copy).then_inc(s["d_copied"], 1)
                for k in range(1, LEVELS):
                    for d in range(2):
                        act.wait_ge(s["y_made"], 10 * h + (2 * (k - 1) + d + 1))
                        if k > 1:
                            act.wait_ge(s["ey_made"], 10 * h + (2 * (k - 2) + d + 1))
                        act_fn(Y_[d].rearrange("p a b -> p (a b)"), bank[3 + d][:, :], ACT.Copy).then_inc(s["y_copied"], 1)
                for i in range(4):
                    act.wait_ge(s["uw_made"], 4 * h + (i + 1))
                    dst = (u_ if i < 2 else w_)[i % 2]
                    act_fn(dst.rearrange("p a b -> p (a b)"), bank[3 + i][:, :], ACT.Copy).then_inc(s["uw_copied"], 1)
                act.wait_ge(s["o_made"], 2 * h + 1)
                act_fn(tmp[0].rearrange("p a b -> p (a b)")[:, 0:SEQ], bank[3][:, 0:SEQ], ACT.Copy).then_inc(s["o_copied"], 1)
            link.leave(HEADS)

            for i in range(4):
                act.wait_ge(s["o_summed"], i + 1)
                rsqrt(r_gdn[:, i, :], bank[4 + i][:, :], 1.0 / P, EPS).then_inc(s["o_rnorm"], 1)
            for j in range(KT):
                act.wait_ge(s["rest_made"], j + 1)
                act_fn(v_rows[:, :, j * P:(j + 1) * P], bank[j % 4][:, 0:SEQ].rearrange("p (a b) -> p a b", a=QT),
                       ACT.Gelu_apprx_tanh).then_inc(s["rest_taken"], 1)
            for j in range(KT):
                act.wait_ge(s["rest_made"], KT + j + 1)
                act_fn(u_cols[:, j, :], bank[j % 4][:, 0:SEQ], ACT.Gelu_apprx_tanh).then_inc(s["rest_taken"], 1)
            for j in range(KT):
                act.wait_ge(s["rest_made"], 2 * KT + j + 1)
                act_fn(z_cols[:, j, :], bank[j % 4][:, 0:SEQ], ACT.Silu).then_inc(s["rest_taken"], 1)
            for j in range(KT):
                act.wait_ge(s["rest_made"], 3 * KT + j + 1)
                act_fn(gate_cols[:, j, :], bank[j % 4][:, :], ACT.Sigmoid).then_inc(s["rest_taken"], 1)
            act.wait_ge(s["v_stats"], 1)
            rsqrt(bn_r[:, :], bn_mv[:, :, 1], 1.0, EPS).then_inc(s["v_rstd"], 1)

            def norm(name, before_it, eps):
                act.wait_ge(s[before_it], KT)
                act_fn(HS, X, ACT.Square).then_inc(s[name + "_ready"], 1)
                act.wait_ge(s[name + "_summed"], 1)
                rsqrt(norm_r, bank[4][:, 0:SEQ], 1.0 / D, eps).then_inc(s[name + "_rnorm"], 1)

            def route(m, experts):
                act.wait_ge(s["route_exp_in"], 2 * m + 1)
                if m == 0:
                    n_ = QT * GROUPS1
                    act_fn(rt[1][:, 0:n_], rt[1][:, 0:n_], ACT.Exp).then_inc(s["route_exp"], 1)
                    act.wait_ge(s["route_exp_in"], 2)
                    act_fn(rt[5][:, :], rt[5][:, :], ACT.Exp).then_inc(s["route_exp"], 1)
                else:
                    n_ = QT * E2
                    act_fn(rt[1][:, 0:n_], rt[1][:, 0:n_], ACT.Exp).then_inc(s["route_exp"], 1)
                act.wait_ge(s["gates_turned"], m + 1)
                act_fn(gate_T[0:experts, :], bank[6][0:experts, 0:SEQ], ACT.Copy).then_inc(s["gates_turned_copied"], 1)
                done = (0, E1 // 2)[m]
                for e in range(0, experts, 2):
                    act.wait_ge(s["gates_spread"], done + e // 2 + 1)
                    act_fn(gate_bc[:, e:e + 2, :].rearrange("p a b -> p (a b)"), bank[(e // 2) % 4][:, :], ACT.Copy
                           ).then_inc(s["gates_spread_copied"], 1)

            def mixture(m, slices):
                def silu(b, made):
                    act.wait_ge(s[f"up_made{m}"], made)
                    act_fn(silu_h[b], bank[2 * b][:, :], ACT.Silu).then_inc(s[f"silu_made{m}"], 1)
                turns = slices // 2
                with act.Fori(0, turns) as i:
                    for b in range(2):
                        silu(b, 2 * i + (b + 1))

            norm("ffn", "residual1", EPS)
            route(0, E1)
            mixture(0, E1 * E1_SUB)
            norm("final", "residual2", EPS)
            for j in range(O20):
                act.wait_ge(s["qkv2_made"], j + 1)
                acc = bank[j % 4]
                part, i = divmod(j, 4)
                if part in (2, 5):
                    dst = (vs if part == 2 else vd2)[:, :, i * P:(i + 1) * P]
                    act_fn(dst, acc[:, 0:SEQ].rearrange("p (a b) -> p a b", a=QT), ACT.Copy).then_inc(s["qkv2_taken"], 1)
                else:
                    dst = {0: qs, 1: ks, 3: qd2, 4: kd2}[part][:, i, :]
                    act_fn(dst, acc[:, 0:SEQ], ACT.Copy, scale=DH2 ** -0.5 if part in (0, 3) else 1.0
                           ).then_inc(s["qkv2_taken"], 1)
            def sb_soft(a):
                act.wait_ge(s["sb_scored"], a + 1)
                b = sc[a % 2]
                b2 = b.rearrange("p a b -> p (a b)")
                if a >= 2:
                    act.wait_ge(s["sb_exponent"], a - 1)
                link(act_fn(b2, bank[a % 2][:, :], ACT.Abs))
                link(act_fn(b2, b2, ACT.Exp, scale=-1.0))
                act_fn(b2, b2, ACT.Ln, bias=eps_ap[1.0]).then_inc(s["sb_soft"], 1)

            def sb_exp(a):
                act.wait_ge(s["sb_exponent"], a + 1)
                act_fn(sc[4 + a % 2], sc[4 + a % 2], ACT.Exp).then_inc(s["sb_exped"], 1)

            for a in range(H2 + 1):
                if a < H2:
                    sb_soft(a)
                if a >= 1:
                    sb_exp(a - 1)

            def dl_exp(a):
                act.wait_ge(s["dl_shifted"], a + 1)
                for qt in range(QT):
                    act_fn(sc[a % 2][:, qt, :], bank[a % 2][:, qt * SEQ:(qt + 1) * SEQ], ACT.Exp, bias=am[:, a % 2, qt:qt + 1]
                           ).then_inc(s["dl_exped"], 1)

            def dl_copy(a):
                act.wait_ge(s["dl_turned"], a + 1)
                if a >= 2:
                    act.wait_ge(s["dl_valued"], a - 1)
                act_fn(sc[4 + a % 2].rearrange("p a b -> p (a b)"), bank[2 + a % 2][:, :], ACT.Copy
                       ).then_inc(s["dl_turned_copied"], 1)

            for a in range(H2 + 1):
                if a < H2:
                    dl_exp(a)
                if a >= 1:
                    dl_copy(a - 1)
            for i in range(4):
                act.wait_ge(s["att_summed"], i + 1)
                rsqrt(r_att[:, i, :], bank[i][:, :], 1.0 / DH2, EPS).then_inc(s["att_rnorm"], 1)

            def layer_norm(name):
                act.wait_ge(s[name + "_mean"], 1)
                act_fn(norm_m, bank[4][:, 0:SEQ], ACT.Copy, scale=1.0 / D).then_inc(s[name + "_mean_copied"], 1)
                act.wait_ge(s[name + "_centred"], 1)
                act_fn(HS, X, ACT.Square).then_inc(s[name + "_sq"], 1)
                act.wait_ge(s[name + "_var"], 1)
                rsqrt(norm_r, bank[5][:, 0:SEQ], 1.0 / D, LN_EPS).then_inc(s[name + "_rnorm"], 1)

            layer_norm("ln1")
            route(1, E2)
            mixture(1, E2 * E2_SUB)
            layer_norm("ln2")

        @block.vector
        def _(dve):
            link = Chain(dve, s["dve_chain"])
            tt_, ts_, stt = nc.vector.tensor_tensor, nc.vector.tensor_scalar, nc.vector.scalar_tensor_tensor
            red, cp = nc.vector.tensor_reduce, nc.vector.tensor_copy

            nc.vector.memset(ones[:, :], 1.0).then_inc(s["ones_set"], 1)
            for value in (EPS, LN_EPS, 1.0):
                nc.vector.memset(eps_ap[value], value).then_inc(s["eps_set"], 1)
            dve.wait_ge(s["vec_landed"], 16)
            dve.wait_ge(s["mod_made"], 1)
            link(tt_(mod[:, :, :], bank[2][:, 0:12 * KT].rearrange("p (a b) -> p a b", b=2), over(V("ada_b"), 2), ALU.add))
            link(stt(mixs[:, :, :], mod[:, KT:2 * KT, :], 1.0, over(V("norm_mix_g"), 2), ALU.add, ALU.mult))
            link(stt(ffns[:, :], mod[:, 4 * KT:5 * KT, 0], 1.0, V("norm_ffn_g"), ALU.add, ALU.mult))
            dve.wait_ge(s["xc_rnorm"], 1)
            link(tt_(hc[:, :, :], xc[:, :, :], times(area(0, 512), KT), ALU.mult))
            for k in range(KT):
                for who, cols in ((1, slice(0, SEQ)), (0, slice(SEQ, TOK))):
                    ins = ts_(hc[:, k, cols], hc[:, k, cols], mixs[:, k, who:who + 1], mod[:, k, who:who + 1],
                              ALU.mult, ALU.add)
                ins.then_inc(s["modulated"], 1)
            for j in range(3):
                nc.vector.memset(pad[j], 0.0).then_inc(s["pads_zeroed"], 1)
            dve.wait_ge(s["ba_made"], 1)
            ba = bank[0][:, 0:TT * 2 * DH].rearrange("p (a b) -> p a b", a=TT)
            link(cp(gates_in[:, :, 0:DH], ba[:, :, 0:DH]))
            tt_(gates_in[:, :, DH:2 * DH], ba[:, :, DH:2 * DH], times(V("dt_bias"), TT), ALU.add).then_inc(s["a_in"], 1)
            dve.wait_ge(s["a_in"], 1)
            dve.wait_ge(s["soft_ready"], 2)
            link(stt(gd["g"][:, :, :], gates_in[:, :, DH:2 * DH], 0.0, gd["t"][:, :, :], ALU.max, ALU.add))
            stt(gd["g"][:, :, :], gd["g"][:, :, :], -1.0, times(gd["kb"][:, 0, :], TT), ALU.mult, ALU.mult
                ).then_inc(s["g_raw"], 1)
            dve.wait_ge(s["cum_made"], 1)
            link(cp(gd["G"][:, :, 0:HEADS], bank[1][:, 0:32].rearrange("p (a b) -> p a b", a=TT)))
            link(cp(gd["G"][:, :, HEADS:DH], bank[1][:, 32:64].rearrange("p (a b) -> p a b", a=TT)))
            tt_(gd["kd"][:, :, :], bank[1][:, 64:128].rearrange("p (a b) -> p a b", a=TT), gd["G"][:, :, :], ALU.subtract
                ).then_inc(s["cum_ready"], 1)
            dve.wait_ge(s["cum_exp"], 2)
            dve.wait_ge(s["beta_ready"], 1)
            link(tt_(gd["kb"][:, :, :], gd["beta"][:, :, :], gd["t"][:, :, :], ALU.mult))
            nc.vector.memset(bn_r[:, :], 0.0).then_inc(s["g_ready"], 1)
            dve.wait_ge(s["g_ready"], 1)
            dve.wait_ge(s["bias_copied"], 1)
            nc.vector.memset(state[0], 0.0).then_inc(s["head_free"], 1)
            dve.wait_ge(s["head_free"], 1)

            with dve.Fori(0, HEADS) as h:
                link.enter(h, 3 * (CONV - 1) + 4)
                for j in range(3):
                    dve.wait_ge(s["padded"], 3 * h + (j + 1))
                    at = h * (3 * CONV) + j * CONV
                    c3 = conv[j].rearrange("p a b -> p (a b)").rearrange("p (a b) -> p a b", a=2)
                    for i in range(CONV):
                        wgt = V("conv_w")[:, bass.ds(at + i, 1)]
                        src = pad[j][:, :, i:i + SEQ]
                        if i == 0:
                            link(ts_(c3, src, wgt, None, ALU.mult))
                        elif i < CONV - 1:
                            link(stt(c3, src, wgt, c3, ALU.mult, ALU.add))
                        else:
                            stt(c3, src, wgt, c3, ALU.mult, ALU.add).then_inc(s["conved"], 1)
                dve.wait_ge(s["norms_ready"], 2 * h + 2)
                tt_(conv[1], conv[1], tmp[1], ALU.mult).then_inc(s["normed"], 1)
                stt(conv[0].rearrange("p a b -> p (a b)"), conv[0].rearrange("p a b -> p (a b)"), float(P) ** -0.5,
                    tmp[0].rearrange("p a b -> p (a b)"), ALU.mult, ALU.mult).then_inc(s["normed"], 1)
                for d in range(2):
                    dve.wait_ge(s["gram"], 8 * h + (d + 1))
                    for a in range(TT):
                        ins = ts_(et[d][:, a, :], bank[1 + d][:, a * P:(a + 1) * P],
                                  gd["G"][:, a, bass.ds(h + HEADS * d, 1)], 0.0, ALU.subtract, ALU.min)
                    ins.then_inc(s["g_diffs"], 1)
                for src, b, dsts in ((gd["kb"], 5, kb), (gd["kd"], 5, kd), (gd["beta"], 6, vb)):
                    dve.wait_ge(s["gram"], 8 * h + b)
                    for d in range(2):
                        tt_(dsts[d], bank[b][:, :].rearrange("p (a b) -> p a b", a=TT),
                            src[:, :, bass.ds(h + HEADS * d, 1)].broadcast_to([P, TT, P]), ALU.mult
                            ).then_inc(s["rows_scaled"], 1)
                for d in range(2):
                    dve.wait_ge(s["masked"], 2 * h + (d + 1))
                    dve.wait_ge(s["gram"], 8 * h + 8)
                    e2 = et[d].rearrange("p a b -> p (a b)")
                    link(tt_(qk[d].rearrange("p a b -> p (a b)"), bank[0][:, :], e2, ALU.mult))
                    link(tt_(e2, bank[3 + d][:, :], e2, ALU.mult))
                    tt_(up[d].rearrange("p a b -> p (a b)"), bank[7][:, :], e2, ALU.mult).then_inc(s["couplings"], 1)
                for d in range(2):
                    dve.wait_ge(s["level_masked"], 12 * h + (d + 1))
                    tt_(E_[d], times(M("ident"), TT), levels[d], ALU.subtract).then_inc(s["first_inverse"], 1)
                for k in range(1, LEVELS):
                    for d in range(2):
                        if k < LEVELS - 1:
                            dve.wait_ge(s["dy_made"], 8 * h + (2 * (k - 1) + d + 1))
                            dd = D_[d].rearrange("p a b -> p (a b)")
                            if k == 1:
                                dve.wait_ge(s["d_copied"], 2 * h + (d + 1))
                            else:
                                dve.wait_ge(s["d_updated"], 8 * h + (2 * (k - 2) + d + 1))
                            tt_(dd, dd, bank[5 + d][:, :], ALU.subtract).then_inc(s["d_updated"], 1)
                        dve.wait_ge(s["ey_made"], 10 * h + (2 * (k - 1) + d + 1))
                        if k == 1:
                            dve.wait_ge(s["first_inverse"], 2 * h + (d + 1))
                        else:
                            dve.wait_ge(s["e_updated"], 10 * h + (2 * (k - 2) + d + 1))
                        ee = E_[d].rearrange("p a b -> p (a b)")
                        tt_(ee, ee, bank[1 + d][:, :], ALU.subtract).then_inc(s["e_updated"], 1)
                n_chunks = TOK // CHUNK
                for n in range(n_chunks):
                    for d in range(2):
                        c, r = chunk_of(n, d)
                        half = slice(r, r + CHUNK)
                        if n > 0:
                            dve.wait_ge(s["ws_made"], 14 * h + (2 * (n - 1) + d + 1))
                            dve.wait_ge(s["uw_copied"], 4 * h + 4)
                            tt_(u_[d][half, c, :], u_[d][half, c, :], bank[(0, 7)[d]][half, 0:P], ALU.subtract
                                ).then_inc(s["v_new"], 1)
                    for d in range(2):
                        c, r = chunk_of(n, d)
                        if n == n_chunks - 1:
                            continue
                        dve.wait_ge(s["kv_made"], 14 * h + (2 * n + d + 1))
                        if n == 0:
                            cp(state[d], bank[1 + d][:, 0:P]).then_inc(s["stepped"], 1)
                        else:
                            dve.wait_ge(s["stepped"], 14 * h + (2 * (n - 1) + d + 1))
                            last = r + CHUNK - 1 if d == 0 else r
                            stt(state[d], state[d], tmp[d][:, c, last:last + 1], bank[1 + d][:, 0:P], ALU.mult, ALU.add
                                ).then_inc(s["stepped"], 1)
                dve.wait_ge(s["o_made"], 2 * h + 2)
                dve.wait_ge(s["o_copied"], h + 1)
                tt_(o_heads[:, bass.ds(h, 1), :].rearrange("p a b -> p (a b)"),
                    tmp[0].rearrange("p a b -> p (a b)")[:, 0:SEQ], bank[4][:, 0:SEQ], ALU.add).then_inc(s["head_free"], 1)
            link.leave(HEADS)

            dve.wait_ge(s["head_free"], HEADS + 1)
            oh = o_heads[:, :, :].rearrange("p a b -> p (a b)")
            tt_(sq_gdn.rearrange("p a b -> p (a b)"), oh, oh, ALU.mult).then_inc(s["o_squared"], 1)
            dve.wait_ge(s["o_rnorm"], 4)
            yg = y_gdn.rearrange("p a b -> p (a b)")
            stt(yg, oh, V("gdn_norm_g"), r_gdn.rearrange("p a b -> p (a b)"), ALU.mult, ALU.mult).then_inc(s["gdn_normed"], 1)
            dve.wait_ge(s["rest_taken"], KT)
            for qt in range(QT):
                for i in range(2):
                    link(nc.vector.bn_stats(bn[:, qt, i, :], v_rows[:, qt, i * 512:(i + 1) * 512]))
                ins = nc.vector.bn_aggr(bn_mv[:, qt, :], bn[:, qt, :, :].rearrange("p a b -> p (a b)"))
                if qt < QT - 1:
                    link(ins)
            ins.then_inc(s["v_stats"], 1)
            dve.wait_ge(s["rest_taken"], 3 * KT)
            dve.wait_ge(s["gdn_normed"], 1)
            link(tt_(yg, yg, z_cols.rearrange("p a b -> p (a b)"), ALU.mult))
            dve.wait_ge(s["v_rstd"], 1)
            dve.wait_ge(s["head_landed"], 16 * (HEADS + 1))
            for qt in range(QT):
                link(ts_(v_rows[:, qt, :], v_rows[:, qt, :], bn_mv[:, qt, 0:1], bn_r[:, qt:qt + 1], ALU.subtract, ALU.mult))
            link(tt_(v_rows, v_rows, times(ln_rows[:, 0, :], QT), ALU.mult))
            tt_(v_rows, v_rows, times(ln_rows[:, 1, :], QT), ALU.add).then_inc(s["v_normed"], 1)
            for j in range(KT):
                dve.wait_ge(s["sgu_mixed"], j + 1)
                tt_(y_sgu[:, j, :], bank[4 + j % 3][:, 0:SEQ], u_cols[:, j, :], ALU.mult).then_inc(s["sgu_taken"], 1)
            for j in range(KT):
                dve.wait_ge(s["rest_made"], 4 * KT + j + 1)
                dve.wait_ge(s["rest_taken"], 4 * KT + j)
                link(tt_(gate_cols[:, j, :], gate_cols[:, j, :], bank[j % 4][:, :], ALU.mult))
                tt_(merged[:, j, :], gate_cols[:, j, 0:SEQ], gate_cols[:, j, SEQ:2 * SEQ], ALU.add
                    ).then_inc(s["rest_taken"], 1)
            for j in range(KT):
                dve.wait_ge(s["rest_made"], 5 * KT + j + 1)
                ins = stt(X[:, j, :], bank[j % 4][:, 0:SEQ], mod[:, 2 * KT + j, 0:1], X[:, j, :], ALU.mult, ALU.add)
                ins.then_inc(s["residual1"], 1)
            dve.wait_ge(s["ffn_rnorm"], 1)
            link(tt_(H, X, times(norm_r, KT), ALU.mult))
            for k in range(KT):
                ts_(H[:, k, :], H[:, k, :], ffns[:, k:k + 1], mod[:, 3 * KT + k, 0:1], ALU.mult, ALU.add
                    ).then_inc(s["route_in0"], 1)

            def route1():
                n = QT
                dve.wait_ge(s["logits_made"], 1)
                ps = bank[5][:, 0:QT * (GROUPS1 + E1)].rearrange("p (a b) -> p a b", a=QT)
                lg = rt[0][:, 0:n * GROUPS1].rearrange("p (a b) -> p a b", a=n)
                le = rt[2][:, :].rearrange("p (a b) -> p a b", a=n)
                gm, pg, m1, m2, sm = (rs[i][:, 0:n] for i in range(5))
                ex = rt[1][:, 0:n * GROUPS1].rearrange("p (a b) -> p a b", a=n)
                hot = rt[3][:, 0:n * GROUPS1]
                link(cp(lg, ps[:, :, 0:GROUPS1]))
                link(cp(le, ps[:, :, GROUPS1:]))
                link(red(gm, lg, AX_X, ALU.max))
                link(tt_(hot.rearrange("p (a b) -> p a b", a=n), lg, over(gm, GROUPS1), ALU.is_equal))
                tt_(ex, lg, over(gm, GROUPS1), ALU.subtract).then_inc(s["route_exp_in"], 1)
                dve.wait_ge(s["route_exp"], 1)
                link(red(sm, ex, AX_X, ALU.add))
                link(nc.vector.reciprocal(pg, sm))
                off = rt[4][:, 0:n * GROUPS1]
                link(ts_(off, hot, -1.0, -NEG, ALU.add, ALU.mult))
                le4 = rt[2][:, :].rearrange("p (a b) -> p a b", b=PER1)
                link(tt_(le4, le4, over(hot, PER1), ALU.mult))
                link(tt_(le4, le4, over(off, PER1), ALU.add))
                link(red(m1, le, AX_X, ALU.max))
                sel2 = rt[6][:, :].rearrange("p (a b) -> p a b", a=n)
                link(tt_(sel2, le, over(m1, E1), ALU.is_equal))
                link(stt(rt[6][:, :], rt[6][:, :], NEG, rt[2][:, :], ALU.mult, ALU.add))
                link(red(m2, sel2, AX_X, ALU.max))
                keep = rt[7][:, :].rearrange("p (a b) -> p a b", a=n)
                link(tt_(keep, le, over(m2, E1), ALU.is_ge))
                dif = rt[5][:, :].rearrange("p (a b) -> p a b", a=n)
                tt_(dif, le, over(m1, E1), ALU.subtract).then_inc(s["route_exp_in"], 1)
                dve.wait_ge(s["route_exp"], 2)
                link(tt_(dif, dif, keep, ALU.mult))
                link(red(sm, dif, AX_X, ALU.add))
                link(nc.vector.reciprocal(gm, sm))
                link(tt_(gm, gm, pg, ALU.mult))
                tt_(gate_rows[:, :, 0:E1], dif, over(gm, E1), ALU.mult).then_inc(s["gates_ready"], 1)

            def route2():
                n = QT
                dve.wait_ge(s["logits_made"], 2)
                ps = bank[5][:, 0:n * E2].rearrange("p (a b) -> p a b", a=n)
                gm, gs = rs[0][:, 0:n], rs[1][:, 0:n]
                ex = rt[1][:, 0:n * E2]
                ex3 = ex.rearrange("p (a b) -> p a b", a=n)
                ex4 = ex.rearrange("p (a b) -> p a b", b=PER2)
                link(red(gm, ps, AX_X, ALU.max))
                tt_(ex3, ps, over(gm, E2), ALU.subtract).then_inc(s["route_exp_in"], 1)
                dve.wait_ge(s["route_exp"], 3)
                m1, m2, sm, hot = (rs[i][:, 0:n * GROUPS2] for i in range(2, 6))
                w = rt[3][:, 0:n * E2]
                w4 = w.rearrange("p (a b) -> p a b", b=PER2)
                link(red(m1, ex4, AX_X, ALU.max))
                link(tt_(w4, ex4, over(m1, PER2), ALU.is_lt))
                link(tt_(w, w, ex, ALU.mult))
                link(red(m2, w4, AX_X, ALU.max))
                link(tt_(sm, m1, m2, ALU.add))
                sm3 = sm.rearrange("p (a b) -> p a b", a=n)
                link(red(gs, sm3, AX_X, ALU.max))
                link(tt_(hot.rearrange("p (a b) -> p a b", a=n), sm3, over(gs, GROUPS2), ALU.is_equal))
                link(tt_(w4, ex4, over(m2, PER2), ALU.is_ge))
                link(tt_(w, w, ex, ALU.mult))
                link(tt_(w4, w4, over(hot, PER2), ALU.mult))
                link(nc.vector.reciprocal(gm, gs))
                tt_(gate_rows[:, :, 0:E2], w.rearrange("p (a b) -> p a b", a=n), over(gm, E2), ALU.mult
                    ).then_inc(s["gates_ready"], 1)

            def mixture(m, slices, sub):
                dve.wait_ge(s["gates_spread_copied"], (E1 // 2, (E1 + E2) // 2)[m])
                for i in range(4):
                    ins = nc.vector.memset(bank[4 + i][:, :], 0.0)
                ins.then_inc(s[f"acc_zeroed{m}"], 1)
                turns = slices // 4
                with dve.Fori(0, turns) as i:
                    link.enter(i, 4)
                    for k in range(4):
                        b = k % 2
                        dve.wait_ge(s[f"silu_made{m}"], 4 * i + (k + 1))
                        link(tt_(silu_h[b], silu_h[b], bank[2 * b + 1][:, :], ALU.mult))
                        e = 4 * i + k if sub == 1 else i
                        gate = gate_bc[:, bass.ds(e, 1), :].broadcast_to([P, 2, SEQ])
                        tt_(hid[b], silu_h[b].rearrange("p (a b) -> p a b", a=2), gate, ALU.mult
                            ).then_inc(s[f"hid_ready{m}"], 1)
                    link.leave(turns)
                dve.wait_ge(slots_used, (MOE1_G, MOE2_G)[m] + slices)

            route1()
            mixture(0, E1 * E1_SUB, E1_SUB)
            for j in range(KT):
                ins = stt(X[:, j, :], bank[4 + j // 2][:, (j % 2) * SEQ:(j % 2 + 1) * SEQ], mod[:, 5 * KT + j, 0:1],
                          X[:, j, :], ALU.mult, ALU.add)
                ins.then_inc(s["residual2"], 1)
            dve.wait_ge(s["final_rnorm"], 1)
            link(tt_(X, X, times(norm_r, KT), ALU.mult))
            tt_(X, X, over(V("final_norm_g"), SEQ), ALU.mult).then_inc(s["x3_ready"], 1)

            dve.wait_ge(s["attn_landed"], 16)
            def sb_logs(a):
                dve.wait_ge(s["sb_soft"], a + 1)
                b = sc[a % 2].rearrange("p a b -> p (a b)")
                lm = sc[2 + a % 2].rearrange("p a b -> p (a b)")
                if a >= 2:
                    dve.wait_ge(s["sb_between"], a - 1)
                z = bank[a % 2][:, :]
                link(stt(b, z, 0.0, b, ALU.min, ALU.subtract))
                link(tt_(lm, b, z, ALU.subtract))
                tt_(lm, lm, before.rearrange("p a b -> p (a b)"), ALU.mult).then_inc(s["sb_logs"], 1)

            def sb_exponent(a):
                dve.wait_ge(s["sb_between"], a + 1)
                if a >= 2:
                    dve.wait_ge(s["sb_valued"], a - 1)
                tt_(sc[4 + a % 2].rearrange("p a b -> p (a b)"), sc[a % 2].rearrange("p a b -> p (a b)"),
                    bank[2 + a % 2][:, :], ALU.add).then_inc(s["sb_exponent"], 1)

            def sb_weights(a):
                dve.wait_ge(s["sb_exped"], a + 1)
                tt_(sc[4 + a % 2], sc[4 + a % 2], before, ALU.mult).then_inc(s["sb_weights"], 1)

            def take(name, a2, first):
                dve.wait_ge(s[f"{name}_valued"], 2 * a2 + 2)
                cp(o_att[:, first + a2, :], bank[4 + a2 % 2][:, 0:SEQ]).then_inc(s[f"{name}_o_taken"], 1)

            dve.wait_ge(s["x3_ready"], 1)
            for a in range(H2 + 1):
                if a < H2:
                    sb_logs(a)
                if a >= 1:
                    sb_exponent(a - 1)
                    sb_weights(a - 1)
                if a >= 4 and a % 2 == 0:
                    take("sb", a // 2 - 2, 0)
            take("sb", 3, 0)

            def dl_shift(a):
                dve.wait_ge(s["dl_scored"], a + 1)
                if a >= 1:
                    dve.wait_ge(s["dl_shifted"], a)
                link(red(am[:, 2, :], bank[a % 2][:, :].rearrange("p (a b) -> p a b", a=QT), AX_X, ALU.max))
                ts_(am[:, a % 2, :], am[:, 2, :], -1.0, None, ALU.mult).then_inc(s["dl_shifted"], 1)

            def dl_probs(a):
                dve.wait_ge(s["dl_exped"], 2 * a + 2)
                if a >= 1:
                    dve.wait_ge(s["dl_probs"], a)
                if a >= 2:
                    dve.wait_ge(s["dl_turned"], a - 1)
                dst = sc[2 + a % 2]
                link(tt_(dst, sc[a % 2], count, ALU.mult))
                link(red(am[:, 2, :], dst, AX_X, ALU.add))
                link(nc.vector.reciprocal(am[:, 3, :], am[:, 2, :]))
                tt_(dst, dst, over(am[:, 3, :], SEQ), ALU.mult).then_inc(s["dl_probs"], 1)

            for a in range(H2 + 1):
                if a < H2:
                    dl_shift(a)
                if a >= 1:
                    dl_probs(a - 1)
                if a >= 4 and a % 2 == 0:
                    take("dl", a // 2 - 2, 4)
            take("dl", 3, 4)
            dve.wait_ge(s["sb_o_taken"], 4)
            dve.wait_ge(s["dl_o_taken"], 4)
            oa = o_att.rearrange("p a b -> p (a b)")
            tt_(sq_att.rearrange("p a b -> p (a b)"), oa, oa, ALU.mult).then_inc(s["att_squared"], 1)
            dve.wait_ge(s["att_rnorm"], 4)
            link(tt_(oa, oa, r_att.rearrange("p a b -> p (a b)"), ALU.mult))
            tt_(o_att, o_att, over(V("g_heads"), SEQ), ALU.mult).then_inc(s["att_normed"], 1)
            for j in range(KT):
                dve.wait_ge(s["out2_made"], j + 1)
                stt(X[:, j, :], X[:, j, :], ALPHA, bank[j % 4][:, 0:SEQ], ALU.mult, ALU.add).then_inc(s["residual3"], 1)

            def layer_norm(name, then):
                dve.wait_ge(s[name + "_mean_copied"], 1)
                tt_(X, X, times(norm_m, KT), ALU.subtract).then_inc(s[name + "_centred"], 1)
                dve.wait_ge(s[name + "_centred"], 1)
                dve.wait_ge(s[name + "_rnorm"], 1)
                link(tt_(X, X, times(norm_r, KT), ALU.mult))
                link(tt_(X, X, over(V(name + "_g"), SEQ), ALU.mult))
                tt_(X, X, over(V(name + "_b"), SEQ), ALU.add).then_inc(s[then], 1)

            layer_norm("ln1", "route_in1")
            route2()
            mixture(1, E2 * E2_SUB, E2_SUB)
            for j in range(KT):
                stt(X[:, j, :], X[:, j, :], ALPHA, bank[4 + j // 2][:, (j % 2) * SEQ:(j % 2 + 1) * SEQ],
                    ALU.mult, ALU.add).then_inc(s["residual4"], 1)
            layer_norm("ln2", "ln2_done")


def by_partition(w):
    return w.reshape(-1, P, w.shape[-1]).transpose(1, 0, 2)


def as_block(w, col):
    return by_partition(w[:, col:col + P]).reshape(P, D)


def lay_out(a):
    a = {k: np.asarray(v) for k, v in a.items()}
    w_in, w_in2 = a["w_in"][0], a["w_in_2"][0]
    col_ba = 3 * D
    col_z = col_ba + 4 * HEADS
    col_u, col_v, col_g = col_z + D, col_z + 2 * D, col_z + 3 * D
    stream = np.zeros((N_GROUPS, P, GROUP), np.float32)

    def put(first_group, j, block):
        at = (j % BLOCKS) * D
        stream[first_group + j // BLOCKS, :, at:at + D] = block

    for j in range(6 * KT):
        put(0, ADA0 + j, as_block(a["ada_w"][0], j * P))
    for j in range(KT):
        put(0, V0 + j, as_block(w_in, col_v + j * P))
        put(0, U0 + j, as_block(w_in, col_u + j * P))
        put(0, Z0 + j, as_block(w_in, col_z + j * P))
        put(0, G0 + 2 * j, as_block(w_in, col_g + j * P))
        put(0, G0 + 2 * j + 1, as_block(w_in, col_g + D + j * P))
        put(0, AB0 + 2 * j, as_block(a["w_branch_a"][0], j * P))
        put(0, AB0 + 2 * j + 1, as_block(a["w_branch_b"][0], j * P))
        put(0, O0 + j, as_block(a["w_out"][0], j * P))
        put(SECOND_G, O20 + j, as_block(a["w_out_2"][0], j * P))
    for j in range(O20):
        put(SECOND_G, j, as_block(w_in2, j * P))

    def experts(first_group, n, sub, w1, w3, w2):
        for e in range(n):
            for i in range(sub):
                f = slice(i * FS, (i + 1) * FS)
                dst = stream[first_group + e * sub + i]
                dst[:, 0:KT * FS] = by_partition(w1[e][:, f]).reshape(P, -1)
                dst[:, KT * FS:2 * KT * FS] = by_partition(w3[e][:, f]).reshape(P, -1)
                dst[:, 2 * KT * FS:] = by_partition(w2[e][f]).reshape(P, -1)

    experts(MOE1_G, E1, E1_SUB, a["expert_w1"][0], a["expert_w3"][0], a["expert_w2"][0])
    experts(MOE2_G, E2, E2_SUB, a["w_gate_2"][0], a["w_up_2"][0], a["w_down_2"][0])

    head_w = np.zeros((HEADS + 1, P, 3 * D), np.float32)
    for h in range(HEADS):
        for j in range(3):
            head_w[h, :, j * D:(j + 1) * D] = as_block(w_in, j * D + h * P)
    head_w[HEADS, :, 0:D] = a["sgu_ln_g"][0][None, :]
    head_w[HEADS, :, D:2 * D] = a["sgu_ln_b"][0][None, :]
    head_w[HEADS, :, 2 * D:] = a["sgu_w"][0].transpose(2, 0, 1).reshape(P, D)

    vec = np.zeros((P, VEC_N), np.float32)

    def cols(v):
        return v.reshape(-1, P).T
    vec[:, VEC["cond"]] = np.stack([cols(a["c"][0]), cols(a["c_ctx"])], 2).reshape(P, -1)
    vec[:, VEC["ada_b"]] = cols(a["ada_b"][0])
    for name in ("norm_mix_g", "gdn_norm_g", "norm_ffn_g"):
        vec[:, VEC[name]] = cols(a[name][0])
    vec[:, VEC["final_norm_g"]] = cols(a["final_norm_g"])
    for name in ("ln1_g", "ln1_b", "ln2_g", "ln2_b"):
        vec[:, VEC[name]] = cols(a[name + "_2"][0])
    vec[:, VEC["g_heads"]] = cols(np.concatenate([a["g_sb_2"][0], a["g_dil_2"][0]]))
    vec[:, VEC["conv_w"]] = a["conv_w"][0].reshape(CONV, 3, HEADS, P).transpose(3, 2, 1, 0).reshape(P, -1)
    vec[:, VEC["dt_bias"]] = a["dt_bias"][0].reshape(1, DH)
    vec[:, VEC["a_log"]] = a["a_log"][0].reshape(1, DH)

    xc = np.concatenate([by_partition(a["ctx"][0].T), by_partition(a["x"][0].T)], 2)
    rows = np.concatenate([a["sgu_b"][0].reshape(-1), a["router_group_b"][0], a["router_expert_b"][0], a["b_router_2"]])
    router1 = np.concatenate([by_partition(a["router_group_w"][0]), by_partition(a["router_expert_w"][0])], 2)
    router_w = np.concatenate([router1.reshape(P, -1), by_partition(a["w_router_2"]).reshape(P, -1)], 1)
    square, attn, onehot = shape_constants()
    return {
        "stream": stream, "head_w": head_w, "vec": vec, "xc": xc, "rows": rows[None, :], "router_w": router_w,
        "ba_w": by_partition(w_in[:, col_ba:col_z]), "square": square, "attn": attn, "onehot": onehot,
        "rel_bias": a["rel_bias_2"],
    }


def kernel(**inputs):
    import concourse.bacc as bacc
    from concourse.bass_utils import run_bass_kernel_spmd

    nc = bacc.Bacc("TRN2", target_bir_lowering=False, num_devices=1)
    arrays = {f"in_{k}": np.ascontiguousarray(v) for k, v in lay_out(inputs).items()}
    t = {k[3:]: nc.dram_tensor(k, v.shape, F32, kind="ExternalInput").ap() for k, v in arrays.items()}
    t["out"] = nc.dram_tensor("out_y", (P, KT, SEQ), F32, kind="ExternalOutput").ap()
    build(nc, t)
    got = run_bass_kernel_spmd(nc, [arrays], core_ids=[0]).results[0]["out_y"]
    return np.ascontiguousarray(np.asarray(got).transpose(2, 1, 0).reshape(1, SEQ, D))
```

```python
from contextlib import ExitStack

import numpy as np

import concourse.bass as bass
from concourse import mybir

F32 = mybir.dt.float32
BF16 = mybir.dt.bfloat16
U32 = mybir.dt.uint32
ALU = mybir.AluOpType
ACT = mybir.ActivationFunctionType
AX_X = mybir.AxisListType.X

P = 128
D = 1024
KT = D // P
SEQ = 256
TOK = 2 * SEQ
QT = SEQ // P
TT = TOK // P
HEADS = 8
DH = 2 * HEADS
CHUNK = 64
CONV = 5
LEVELS = 6
EPS = 1e-6
LN_EPS = 1e-5
ALPHA = 2.0 ** 0.25
NEG = -1e30
E1, E1_SUB = 32, 1
E2, E2_SUB = 16, 4
GROUPS1, PER1 = 4, 8
GROUPS2, PER2 = 4, 4
SKIP = 4096
NB = 3
FS = 256
H2 = 8
DH2 = 64
BUCKETS = 32
BIAS_W = 2 * SEQ

RING = 3
BLOCKS = 6
ADA_BLOCKS = BLOCKS // 2
GROUP = BLOCKS * D

ADA0 = 0
V0 = ADA0 + 6 * KT
U0 = V0 + KT
Z0 = U0 + KT
G0 = Z0 + KT
AB0 = G0 + 2 * KT
O0 = AB0 + 2 * KT
N_FIRST = O0 + KT
QS0, KS0, VS0, QD0, KD0, VD0, O20 = 0, 4, 8, 12, 16, 20, 24
N_SECOND = O20 + KT
FIRST_GROUPS = -(-N_FIRST // BLOCKS)
SECOND_GROUPS = -(-N_SECOND // BLOCKS)
MOE1_G = FIRST_GROUPS
SECOND_G = MOE1_G + E1 * E1_SUB
MOE2_G = SECOND_G + SECOND_GROUPS
N_GROUPS = MOE2_G + E2 * E2_SUB


def layout(*fields):
    at, out = 0, {}
    for name, n in fields:
        out[name] = slice(at, at + n)
        at += n
    return out, at


ROWS_N = D + GROUPS1 + E1 + E2

VEC, VEC_N = layout(
    ("cond", KT * 2), ("ada_b", 6 * KT), ("norm_mix_g", KT), ("conv_w", 3 * KT * CONV), ("gdn_norm_g", 1),
    ("norm_ffn_g", KT), ("final_norm_g", KT), ("ln1_g", KT), ("ln1_b", KT), ("ln2_g", KT), ("ln2_b", KT),
    ("g_heads", KT), ("token", QT), ("dt_bias", DH), ("a_log", DH))
MATS = ["ident", "tri_f", "tri_b", "same"] + [f"level{k}_{d}" for k in range(LEVELS) for d in "fb"]


def shape_constants():
    s, t = np.arange(P)[:, None], np.arange(P)[None, :]
    same = s // CHUNK == t // CHUNK
    mats = {"ident": s == t, "tri_f": same & (s <= t), "tri_b": same & (s >= t), "same": same}
    for k in range(LEVELS):
        b = 1 << k
        up = (s // (2 * b) == t // (2 * b)) & (s // b < t // b)
        mats[f"level{k}_f"], mats[f"level{k}_b"] = up, up.T
    square = np.stack([mats[n] for n in MATS], 1).astype(np.float32)
    q = np.arange(SEQ)
    before = (np.arange(P)[:, None, None] + P * np.arange(QT)[None, :, None]) < q[None, None, :]
    after = s > t
    def count(d):
        return ((d >= 0) & (d <= 128)) * 1 + ((d >= 0) & (d % 4 == 0) & (d <= 512)) + ((d >= 0) & (d % 16 == 0))
    d = (np.arange(P)[:, None, None] + P * np.arange(QT)[None, :, None]) - q[None, None, :]
    attn = np.concatenate([before.reshape(P, -1), count(d).reshape(P, -1), after, s + t == P - 1, s < t, t + 0 * s], 1).astype(np.float32)
    dist = SEQ - 1 - np.arange(BIAS_W)
    half = BUCKETS // 2
    large = half + (np.log(np.maximum(dist, 1).astype(np.float32) / np.float32(half))
                    / np.float32(np.log(2048 / half)) * np.float32(BUCKETS - half)).astype(np.int32)
    bucket = np.where(dist < half, dist, np.minimum(large, BUCKETS - 1))
    bucket = np.where(count(dist) > 0, bucket, BUCKETS)
    onehot = (np.arange(BUCKETS + 1)[:, None] == bucket[None, :]).astype(np.float32)
    return square, attn, onehot


class Chain:

    def __init__(self, engine, sem):
        self.engine, self.sem, self.n, self.step, self.per = engine, sem, 0, None, 0

    def __call__(self, instruction):
        self.n += 1
        instruction.then_inc(self.sem, 1)
        self.engine.wait_ge(self.sem, self.n if self.step is None else self.start + self.step * self.per + self.n)

    def enter(self, step, per):
        self.start, self.step, self.per, self.n = self.n, step, per, 0

    def leave(self, turns):
        assert self.n == self.per, (self.n, self.per)
        self.n, self.step = self.start + turns * self.per, None


def chunk_of(n, d):
    per = SEQ // CHUNK
    seq, i = divmod(n, per)
    c = seq * per + (i if d == 0 else per - 1 - i)
    return c // 2, (c % 2) * CHUNK


def build(nc, t):
    ctx = ExitStack()
    with ctx:
        def sb(name, *shape):
            return ctx.enter_context(nc.sbuf_tensor(name, [P, *shape], F32))

        def sem(name):
            return ctx.enter_context(nc.semaphore(name))

        ring = sb("ring", RING, GROUP)
        head_w = sb("head_w", 3, KT, P)
        xc = sb("xc", KT, TOK)
        hc = sb("hc", KT, TOK)
        o_heads = sb("o_heads", HEADS, SEQ)
        mats = sb("mats", len(MATS), P)
        ones = sb("ones", P)
        vec = sb("vec", VEC_N)
        ba_w = sb("ba_w", KT, 2 * DH)
        arena = sb("arena", 33 * 512)
        cs = sb("cs", KT, 2)
        mod = sb("mod", 6 * KT, 2)
        mixs = sb("mixs", KT, 2)
        ffns = sb("ffns", KT)
        gates_in = sb("gates_in", TT, 2 * DH)
        gd = {n: sb(f"gd_{n}", TT, DH) for n in ("beta", "g", "G", "kb", "kd", "t")}
        bank = [ctx.enter_context(nc.psum_tensor(f"bank{i}", [P, 512], F32)) for i in range(8)]
        token_dram = [nc.dram_tensor(f"token_rows{m}", (SEQ, D), F32, kind="Internal").ap() for m in range(2)]
        pair_dram = [nc.dram_tensor(f"pair_rows{m}", (2 * SEQ, D), F32, kind="Internal").ap() for m in range(2)]
        bias_dram = nc.dram_tensor("bias_rows", (H2, BIAS_W), F32, kind="Internal").ap()

        X, H = xc[:, :, SEQ:TOK], hc[:, :, SEQ:TOK]
        XS, HS = xc[:, :, 0:SEQ], hc[:, :, 0:SEQ]

        def M(name):
            return mats[:, MATS.index(name), :]

        def V(name):
            return vec[:, VEC[name]]

        def area(at, *shape):
            n = int(np.prod(shape))
            a = arena[:, at:at + n]
            if len(shape) == 2:
                return a.rearrange("p (a b) -> p a b", a=shape[0])
            if len(shape) == 3:
                return a.rearrange("p (a b c) -> p a b c", a=shape[0], b=shape[1])
            return a

        def over(ap, n):
            return ap.unsqueeze(len(ap.shape)).broadcast_to([*ap.shape, n])

        def times(ap, n):
            return ap.unsqueeze(1).broadcast_to([ap.shape[0], n, *ap.shape[1:]])

        def place(i):
            return area(512 * i, TT, P)
        conv = [place(0), place(1), place(2)]
        tmp = [place(3), place(4)]
        rhs = [place(5), place(6), place(7), place(8)]
        levels = rhs
        vb, kb, kd = [place(9), place(10)], [place(11), place(12)], [place(13), place(14)]
        et, qd, qk = [place(15), place(16)], [place(17), place(18)], [place(19), place(20)]
        up = [place(21), place(22)]
        E_, D_, Y_ = [place(23), place(24)], [place(25), place(26)], [place(27), place(28)]
        pad = [area(512 * 29 + 520 * j, 2, SEQ + 4) for j in range(3)]
        state = [area(512 * 29 + 1560 + P * d, P) for d in range(2)]
        u_, w_ = D_, Y_
        norms = up
        PROJECTED = (0, 7, 5)

        ada_rows = area(1024, 6 * D)
        v_rows, u_cols, z_cols = area(0, QT, D), area(2048, KT, SEQ), area(4096, KT, SEQ)
        gate_cols = area(6144, KT, 2 * SEQ)
        y_gdn, y_sgu, merged = area(10240, KT, SEQ), area(12288, KT, SEQ), area(14336, KT, SEQ)
        r_gdn = area(12288, 4, 512)
        sq_gdn = area(14336, 4, 512)
        hw = head_w[:, :, :, :].rearrange("p a k n -> p (a k n)")
        ln_rows = hw[:, 0:2 * D].rearrange("p (a n) -> p a n", a=2)
        sgu_wT = hw[:, 2 * D:3 * D].rearrange("p (g n) -> p g n", g=KT)
        bn = sb("bn", QT, 2, 6)
        bn_mv = sb("bn_mv", QT, 2)
        bn_r = sb("bn_r", QT)
        one_row = sb("one_row", 1, ROWS_N)
        eps = sb("eps", 3)
        eps_ap = {EPS: eps[:, 0:1], LN_EPS: eps[:, 1:2], 1.0: eps[:, 2:3]}

        x_rows = [area(D * i, D) for i in range(NB)]
        x_cols = [area(NB * D + D * i, KT, P) for i in range(NB)]
        y_rows = [area(2 * NB * D + D * i, D) for i in range(NB)]
        own_rows = area(NB * D, QT, D)
        act_h = [area(3 * NB * D + FS * i, FS) for i in range(2)]
        hid = [area(3 * NB * D + 2 * FS + FS * i, FS) for i in range(2)]
        hid_T = [area(3 * NB * D + 4 * FS + FS * i, 2, P) for i in range(2)]
        y_all = area(0, 2 * QT, D)
        y_sum = area(2 * QT * D, QT, D)
        norm_r = area(10240, SEQ)
        norm_m = area(10496, SEQ)
        router_w = [area(10752, KT, GROUPS1 + E1), area(10752 + KT * (GROUPS1 + E1), KT, E2)]
        rt = [area(11264 + 64 * i, 2 * 32) for i in range(10)]
        rs = [area(12032 + 16 * i, 16) for i in range(10)]
        gate_rows = area(12288, QT, E1)
        keep = area(12352, QT, E1)
        position = area(12416, QT, E1)
        facts = area(12480, 96).bitcast(BF16).rearrange("p (a b c) -> p a b c", a=QT, b=E1)
        second = area(12576, QT, E1)
        choice_gates = area(12640, 2, QT)
        lists_f = area(12656, 2 * E1)
        idx_token = area(12720, E1).bitcast(U32)
        idx_pair = area(12752, E1).bitcast(U32)
        most = area(12784, 1).bitcast(U32)
        onehot_slots = area(12800, 4096).bitcast(BF16).rearrange("p (a b c) -> p a b c", a=QT, b=E1)
        qs, ks, vs = area(0, 4, SEQ), area(1024, 4, SEQ), area(2048, QT, 512)
        qd2, kd2, vd2 = area(3072, 4, SEQ), area(4096, 4, SEQ), area(5120, QT, 512)
        o_att = area(6144, KT, SEQ)
        bias2 = area(8192, H2, QT, SEQ)
        sc = [area(12288 + 512 * i, QT, SEQ) for i in range(6)]
        sd = [area(12288 + 512 * i, QT, SEQ) if i < 9
              else hw[:, 512 * (i - 6):512 * (i - 5)].rearrange("p (a n) -> p a n", a=QT) for i in range(6, 12)]
        Z_BANKS, SCORE_BANKS = (0, 6), (1, 7)
        sq_att = area(0, 4, 512)
        r_att = area(2048, 4, 512)
        am = sb("am", 4, QT)
        attn_c = hw
        before = attn_c[:, 0:512].rearrange("p (a n) -> p a n", a=QT)
        count = attn_c[:, 512:1024].rearrange("p (a n) -> p a n", a=QT)
        after = attn_c[:, 1024:1024 + P]
        flip = attn_c[:, 1024 + P:1024 + 2 * P]
        earlier = attn_c[:, 1024 + 2 * P:1024 + 3 * P]
        slot_numbers = attn_c[:, 1024 + 3 * P:1024 + 4 * P]
        rel = o_heads[0:BUCKETS + 1, 0, 0:H2]
        onehot = o_heads[0:BUCKETS + 1, 1:3, :].rearrange("p a n -> p (a n)")
        bias_row = o_heads[0:H2, 3:5, :].rearrange("p a n -> p (a n)")

        S = {}

        class Sems:
            def __getitem__(self, name):
                if name not in S:
                    S[name] = sem(name)
                return S[name]
        s = Sems()
        landed = [sem(f"slot{i}_landed") for i in range(RING)]
        slots_used = sem("slots_used")
        landed2 = [[sem(f"second_landed{m}_{i}") for i in range(RING)] for m in range(2)]
        used2 = sem("second_used")

        def group_view(g):
            return ring[:, g % RING, :]

        def block_view(first_group, j):
            g = first_group + j // BLOCKS
            at = (j % BLOCKS) * D
            return ring[:, g % RING, at:at + D].rearrange("p (k n) -> p k n", k=KT)

        SHAPES = ((E1, E1_SUB, MOE1_G), (E2, E2_SUB, MOE2_G))

        def steps_per_turn(sub):
            return 2 * NB if sub == 1 else NB * sub

        def experts_before(m, r):
            return m * 2 * E1 + r * SHAPES[m][0]

        def slices_before(m, r):
            return m * 2 * E1 * E1_SUB + r * SHAPES[m][0] * SHAPES[m][1]

        def made_good(engine, m, counts):
            with engine.If(overflow(engine, m) == 0):
                for sem_, before_it, n in counts:
                    if before_it > 0:
                        engine.wait_ge(sem_, before_it)
                    engine.sem_inc(sem_, n)

        def overflow(engine, m):
            engine.wait_ge(s["counted"], m + 1)
            return engine.value_load(most[0:1, :], min_val=0, max_val=SEQ) > P

        block = ctx.enter_context(nc.Block())

        @block.sync
        def _(sp):
            sp.dma_start(vec[:, :], t["vec"]).then_inc(s["vec_landed"], 16)
            sp.dma_start(xc[:, :, :], t["xc"]).then_inc(s["xc_landed"], 16)
            sp.dma_start(mats[:, :, :], t["square"]).then_inc(s["mats_landed"], 16)

            def load(i, g, landed_, used, used_count):
                if used_count is not None:
                    sp.wait_ge(used, used_count)
                sp.dma_start(ring[:, g % RING, :], t["stream"][bass.ds(RING * i + g, 1)].rearrange("a p n -> (a p) n")
                             ).then_inc(landed_[g % RING], 16)

            def stream(first, end):
                turns = (end - first) // RING
                with sp.Fori(0, turns) as i:
                    for k in range(RING):
                        load(i, first + k, landed, slots_used, RING * i + (first + k - RING + 1))
                for g in range(first + RING * turns, end):
                    load(0, g, landed, slots_used, g - RING + 1)

            def second_pass(m):
                experts, sub, g0 = SHAPES[m]
                n = experts * sub
                used = m * SHAPES[0][0] * SHAPES[0][1]
                with sp.If(overflow(sp, m)):
                    sp.wait_ge(slots_used, g0 + n)
                    for g in range(RING):
                        load(0, g0 + g, landed2[m], used2, None)
                    turns = (n - RING) // RING
                    with sp.Fori(0, turns) as i:
                        for k in range(RING):
                            load(i, g0 + RING + k, landed2[m], used2, RING * i + (used + k + 1))
                    for k in range(RING * (turns + 1), n):
                        load(0, g0 + k, landed2[m], used2, used + k - RING + 1)
                    sp.wait_ge(used2, used + n)

            for g in range(RING):
                load(0, g, landed, slots_used, None)
            stream(RING, SECOND_G)
            second_pass(0)
            load(0, SECOND_G, landed, slots_used, SECOND_G - RING + 1)
            sp.wait_ge(s["y_loaded"], 16)
            stream(SECOND_G + 1, N_GROUPS)
            second_pass(1)
            sp.wait_ge(s["ln2_done"], KT)
            sp.dma_start(t["out"], X).then_inc(s["stored"], 16)
            sp.wait_ge(s["stored"], 16)

        @block.gpsimd
        def _(pool):
            nc.gpsimd.memset(o_heads[BUCKETS:BUCKETS + 1, 0, 0:H2], NEG).then_inc(s["rel_set"], 1)
            pool.dma_start(o_heads[0:BUCKETS, 0, 0:H2], t["rel_bias"]).then_inc(s["tables_landed"], 16)
            pool.dma_start(onehot, t["onehot"]).then_inc(s["tables_landed"], 16)
            pool.dma_start(ba_w[:, :, :], t["ba_w"]).then_inc(s["tables_landed"], 16)
            pool.dma_start(one_row[0:1, 0, :], t["rows"]).then_inc(s["tables_landed"], 16)
            pool.dma_start(hw, t["head_w"][0]).then_inc(s["head_landed"], 16)
            pool.wait_ge(s["bias_copied"], 1)
            pool.dma_start(bias_dram, bias_row).then_inc(s["bias_stored"], 16)
            link = Chain(pool, s["pool_chain"])
            pool.wait_ge(s["g_ready"], 1)
            pool.wait_ge(s["mats_landed"], 16)
            pool.wait_ge(s["bias_stored"], 16)
            with pool.Fori(0, HEADS) as h:
                pool.wait_ge(s["projected"], 3 * h + 3)
                pool.dma_start(hw,
                               t["head_w"][bass.ds(h + 1, 1)].rearrange("a p n -> (a p) n")
                               ).then_inc(s["head_landed"], 16)
                pool.wait_ge(s["head_free"], h + 1)
                for d in range(2):
                    col = bass.ds(h + HEADS * d, 1)
                    tri = M("tri_f" if d == 0 else "tri_b")
                    nc.gpsimd.tensor_tensor(rhs[d], times(tri, TT), gd["g"][:, :, col].broadcast_to([P, TT, P]),
                                            ALU.mult).then_inc(s["rhs_ready"], 1)
                for d in range(2):
                    col = bass.ds(h + HEADS * d, 1)
                    nc.gpsimd.tensor_tensor(rhs[2 + d], times(M("ident"), TT),
                                            gd["beta"][:, :, col].broadcast_to([P, TT, P]),
                                            ALU.mult).then_inc(s["rhs_ready"], 1)
                pool.wait_ge(s["gram"], 8 * h + 4)
                for k in range(1, LEVELS):
                    for d in range(2):
                        if k == 1:
                            pool.wait_ge(s["couplings"], 2 * h + (d + 1))
                        elif k > 2:
                            pool.wait_ge(s["y_made"], 10 * h + (2 * (k - 3) + d + 1))
                        nc.gpsimd.tensor_tensor(levels[2 * (k % 2) + d], up[d], times(M(f"level{k}_{'fb'[d]}"), TT),
                                                ALU.mult).then_inc(s["level_masked"], 1)
                    if k == 2:
                        for d in range(2):
                            pool.wait_ge(s["rows_scaled"], 8 * h + (d + 7))
                            nc.gpsimd.tensor_tensor(qk[d], qk[d], times(M("tri_f" if d == 0 else "tri_b"), TT),
                                                    ALU.mult).then_inc(s["masked"], 1)
                        for d in range(2):
                            pool.wait_ge(s["exp_g"], 2 * h + (d + 1))
                            pool.wait_ge(s["normed"], 2 * h + 2)
                            nc.gpsimd.tensor_tensor(qd[d], conv[0], tmp[d], ALU.mult).then_inc(s["q_decayed"], 1)

            def mixture_pass(m, r):
                experts = SHAPES[m][0]
                eb = experts_before(m, r)
                moved = s[f"moved{m}{r}"]
                n = 0

                def gather(e):
                    nonlocal n
                    if e >= NB:
                        pool.wait_ge(s["x_turned"], eb + e - NB + 1)
                    pool.indirect_dma_start(
                        x_rows[e % NB], None, token_dram[m], bass.IndirectOffsetOnAxis(idx_token[:, e:e + 1], 0),
                        bounds_check=SEQ - 1, oob_is_err=False).then_inc(moved, 16)
                    n += 16
                    pool.wait_ge(moved, n)
                    pool.sem_inc(s["x_gathered"], 1)

                def scatter(e):
                    nonlocal n
                    pool.wait_ge(s["y_ready"], 2 * (eb + e + 2))
                    pool.indirect_dma_start(
                        pair_dram[m], bass.IndirectOffsetOnAxis(idx_pair[:, e:e + 1], 0), y_rows[e % NB], None,
                        bounds_check=2 * SEQ - 1, oob_is_err=False).then_inc(moved, 16)
                    n += 16
                    pool.wait_ge(moved, n)
                    pool.sem_inc(s["y_free"], 1)

                pool.wait_ge(s["lists"], 2 * m + r + 1)
                for e in range(NB):
                    gather(e)
                for e in range(experts):
                    if e + NB < experts:
                        gather(e + NB)
                    scatter(e)

            def mixture(m):
                pool.wait_ge(s["rows_copied"], 4 * (m + 1))
                pool.dma_start(token_dram[m].rearrange("(a p) n -> p a n", p=P), own_rows).then_inc(s["rows_stored"], 16)
                for b in range(NB):
                    nc.gpsimd.memset(x_rows[b], 0.0).then_inc(s["x_rows_cleared"], 1)
                pool.wait_ge(s["rows_stored"], 16 * (m + 1))
                pool.wait_ge(s["x_rows_cleared"], NB * (m + 1))
                mixture_pass(m, 0)
                with pool.If(overflow(pool, m)):
                    mixture_pass(m, 1)
                if m == 0:
                    made_good(pool, 0, [(s["x_gathered"], E1, E1), (s["y_free"], NB + E1, E1)])
                pool.dma_start(y_all, pair_dram[m].rearrange("(a p) n -> p a n", p=P)).then_inc(s["y_loaded"], 16)

            pool.wait_ge(s["residual"], KT)
            pool.dma_start(arena[:, 10752:10752 + KT * (GROUPS1 + E1 + E2)], t["router_w"]).then_inc(s["router_landed"], 16)
            pool.dma_start(hw[:, 0:1024 + 4 * P], t["attn"]).then_inc(s["attn_landed"], 16)
            pool.sem_inc(s["y_free"], NB)
            mixture(0)
            pool.wait_ge(s["x3_ready"], 1)
            for qt in range(QT):
                rows = bass.AP(tensor=bias_dram.tensor, offset=SEQ - P - qt * P, ap=[[1, P], [BIAS_W, H2], [1, SEQ]])
                pool.dma_start(bias2[:, :, qt, :], rows).then_inc(s["bias_landed"], 16)
            pool.wait_ge(s["bias_landed"], 32)
            pool.wait_ge(s["residual"], 3 * KT)
            pool.dma_start(arena[:, 10752:10752 + KT * (GROUPS1 + E1 + E2)], t["router_w"]).then_inc(s["router_landed"], 16)
            mixture(1)

        @block.tensor
        def _(pe):
            def mm(out, lhsT, rhs_, start=True, stop=True, **kw):
                return nc.tensor.matmul(out, lhsT, rhs_, start=start, stop=stop, **kw)

            group_ended = False

            def release(ins):
                nonlocal group_ended
                if group_ended:
                    ins.then_inc(slots_used, 1)
                group_ended = False

            def block_of(first_group, j, last):
                g = first_group + j // BLOCKS
                if j % BLOCKS == 0:
                    pe.wait_ge(landed[g % RING], 16 * (g // RING + 1))
                return block_view(first_group, j)

            def block_ends(j, last):
                nonlocal group_ended
                group_ended = j % BLOCKS == BLOCKS - 1 or j == last

            def project(bank_ap, w, moving, ks=KT, **kw):
                for k in range(ks):
                    ins = mm(bank_ap, w[:, k, :], moving[:, k, :], k == 0, k == ks - 1, **kw)
                    if k == 0:
                        release(ins)
                return ins

            def project_rows(acc, w, src, first):
                for qt in range(QT):
                    for k in range(KT):
                        at = first + qt * P
                        ins = mm(acc[:, qt * P:(qt + 1) * P], src[:, k, at:at + P], w[:, k, :], k == 0, k == KT - 1)
                        if k == 0:
                            release(ins)
                return ins

            def column_sum(out, src, n=KT):
                for k in range(n):
                    ins = mm(out, ones[:, :], src[:, k, :], k == 0, k == n - 1)
                    if k == 0:
                        release(ins)
                return ins

            pe.wait_ge(s["constants_set"], 4)
            pe.wait_ge(s["xc_squared"], 1)
            column_sum(bank[1][:, :], hc).then_inc(s["xc_summed"], 1)
            pe.wait_ge(s["cond_ready"], 1)
            halves = 6 * KT // ADA_BLOCKS
            for i in range(halves + 1):
                if i < halves:
                    j = i * ADA_BLOCKS
                    if i >= 2:
                        pe.wait_ge(s["ada_copied"], i - 1)
                    block_of(0, j, N_FIRST - 1)
                    at = (j % BLOCKS) * D
                    w = ring[:, (j // BLOCKS) % RING, at:at + ADA_BLOCKS * D].rearrange("p (b k n) -> p b k n", b=ADA_BLOCKS, k=KT)
                    for k in range(KT):
                        ins = mm(bank[3 + i % 2][0:2, 0:ADA_BLOCKS * P], cs[:, k, :], w[:, :, k, :], k == 0, k == KT - 1)
                        if k == 0:
                            release(ins)
                    ins.then_inc(s["ada_made"], 1)
                    block_ends(j + ADA_BLOCKS - 1, N_FIRST - 1)
                if i == 0:
                    pe.wait_ge(s["mats_landed"], 16)
                else:
                    pe.wait_ge(s["ada_copied"], i)
                    for b in range(ADA_BLOCKS):
                        j = (i - 1) * ADA_BLOCKS + b
                        ins = nc.tensor.transpose(bank[2][:, 2 * j:2 * j + 2], ada_rows[0:2, j * P:(j + 1) * P],
                                                  M("ident")[0:2, 0:2])
                        release(ins)
            ins.then_inc(s["mod_made"], 1)
            pe.wait_ge(s["tables_landed"], 64)
            pe.wait_ge(s["rel_set"], 1)
            mm(bank[5][0:H2, :], rel, onehot).then_inc(s["bias_made"], 1)
            def project_head(h, first, n):
                if first == 0:
                    pe.wait_ge(s["head_landed"], 16 * h + 16)
                for i in range(first, first + n):
                    j, k = divmod(i, KT)
                    if j == 0 and type(h) is int:
                        pe.wait_ge(s["modulated"], k + 1)
                    ins = mm(bank[PROJECTED[j]][:, :], head_w[:, j, k, :], hc[:, k, :], k == 0, k == KT - 1)
                    if k == KT - 1:
                        ins.then_inc(s["projected"], 1)

            project_head(0, 0, KT)
            pe.wait_ge(s["modulated"], KT)
            pe.wait_ge(s["tables_landed"], 64)
            for tt in range(TT):
                for k in range(KT):
                    ins = mm(bank[3][:, tt * 2 * DH:(tt + 1) * 2 * DH], hc[:, k, tt * P:(tt + 1) * P], ba_w[:, k, :],
                             k == 0, k == KT - 1)
                    release(ins)
            ins.then_inc(s["ba_made"], 1)
            project_head(0, KT, KT)
            pe.wait_ge(s["g_raw"], 1)
            pe.wait_ge(s["mats_landed"], 16)
            g = gd["g"]
            mm(bank[1][:, 0:32].rearrange("p (a b) -> p a b", a=TT), M("tri_f"), g[:, :, 0:HEADS])
            mm(bank[1][:, 32:64].rearrange("p (a b) -> p a b", a=TT), M("tri_b"), g[:, :, HEADS:DH])
            mm(bank[1][:, 64:128], M("same"), g[:, :, :].rearrange("p a b -> p (a b)")).then_inc(s["cum_made"], 1)

            def head(h, last):
                pe.wait_ge(s["head_free"], h + 1)
                for j in range(2):
                    pe.wait_ge(s["squared"], 2 * h + (j + 1))
                    mm(bank[3 + j][:, :], ones[:, :], norms[j].rearrange("p a b -> p (a b)")).then_inc(s["sq_summed"], 1)
                pe.wait_ge(s["rhs_ready"], 4 * h + 4)
                for d in range(2):
                    mm(bank[1 + d][:, :], ones[:, :], rhs[d].rearrange("p a b -> p (a b)")).then_inc(s["gram"], 1)
                pe.wait_ge(s["norms_ready"], 2 * h + 2)
                for d in range(2):
                    mm(bank[3 + d][:, :], ones[:, :], rhs[2 + d].rearrange("p a b -> p (a b)")).then_inc(s["gram"], 1)
                pe.wait_ge(s["padded"], 3 * h + 3)
                pe.wait_ge(s["normed"], 2 * h + 1)
                for a in range(TT):
                    ins = nc.tensor.transpose(bank[5][:, a * P:(a + 1) * P], conv[1][:, a, :], M("ident"))
                ins.then_inc(s["gram"], 1)
                for a in range(TT):
                    ins = mm(bank[7][:, a * P:(a + 1) * P], conv[1][:, a, :], conv[1][:, a, :])
                ins.then_inc(s["gram"], 1)
                pe.wait_ge(s["normed"], 2 * h + 2)
                for a in range(TT):
                    ins = mm(bank[0][:, a * P:(a + 1) * P], conv[1][:, a, :], conv[0][:, a, :])
                ins.then_inc(s["gram"], 1)
                pe.wait_ge(s["activated"], 3 * h + 3)
                for a in range(TT):
                    ins = nc.tensor.transpose(bank[6][:, a * P:(a + 1) * P], conv[2][:, a, :], M("ident"))
                ins.then_inc(s["gram"], 1)
                for d in range(2):
                    pe.wait_ge(s["first_inverse"], 2 * h + (d + 1))
                    pe.wait_ge(s["exp_g"], 2 * h + 2)
                    for a in range(TT):
                        ins = nc.tensor.transpose(bank[1 + d][:, a * P:(a + 1) * P], E_[d][:, a, :], M("ident"))
                    ins.then_inc(s["inverse_turned"], 1)
                for k in range(1, LEVELS):
                    for d in range(2):
                        pe.wait_ge(s["level_masked"], 10 * h + (2 * (k - 1) + d + 1))
                        if k == 1:
                            pe.wait_ge(s["d_copied"], 2 * h + (d + 1))
                        else:
                            pe.wait_ge(s["d_updated"], 8 * h + (2 * (k - 2) + d + 1))
                            pe.wait_ge(s["y_copied"], 10 * h + (2 * (k - 2) + d + 1))
                        for a in range(TT):
                            ins = mm(bank[3 + d][:, a * P:(a + 1) * P], levels[2 * (k % 2) + d][:, a, :], D_[d][:, a, :])
                        ins.then_inc(s["y_made"], 1)

                    def times_y(d):
                        for a in range(TT):
                            ins = mm(bank[5 + d][:, a * P:(a + 1) * P], E_[d][:, a, :], Y_[d][:, a, :])
                        ins.then_inc(s["dy_made"], 1)

                    for d in range(2):
                        pe.wait_ge(s["y_copied"], 10 * h + (2 * (k - 1) + d + 1))
                        if k > 1:
                            pe.wait_ge(s["e_updated"], 10 * h + (2 * (k - 2) + d + 1))
                        if 1 < k < LEVELS - 1:
                            times_y(d)
                        for a in range(TT):
                            ins = mm(bank[1 + d][:, a * P:(a + 1) * P], Y_[d][:, a, :], E_[d][:, a, :])
                        ins.then_inc(s["ey_made"], 1)
                    if k == 1:
                        pe.wait_ge(s["rows_scaled"], 8 * h + 6)
                        for d in range(2):
                            times_y(d)
                for d in range(2):
                    pe.wait_ge(s["e_updated"], 10 * h + (2 * (LEVELS - 2) + d + 1))
                    for a in range(TT):
                        ins = mm(bank[3 + d][:, a * P:(a + 1) * P], E_[d][:, a, :], vb[d][:, a, :])
                    ins.then_inc(s["uw_made"], 1)
                for d in range(2):
                    for a in range(TT):
                        ins = mm(bank[5 + d][:, a * P:(a + 1) * P], kb[d][:, a, :], E_[d][:, a, :])
                    ins.then_inc(s["uw_made"], 1)
                n_chunks = TOK // CHUNK
                at = 0

                def fill(n):
                    nonlocal at
                    n = 0 if last else min(n, 3 * KT - at)
                    if n > 0:
                        project_head(h + 1, at, n)
                        at += n

                for n in range(n_chunks):
                    for d in range(2):
                        c, r = chunk_of(n, d)
                        half = slice(r, r + CHUNK)
                        if n == 0:
                            pe.wait_ge(s["uw_copied"], 4 * h + 4)
                            pe.wait_ge(s["q_decayed"], 2 * h + 2)
                            pe.wait_ge(s["rows_scaled"], 8 * h + 8)
                            pe.wait_ge(s["masked"], 2 * h + 2)
                        else:
                            pe.wait_ge(s["stepped"], 14 * h + (2 * (n - 1) + d + 1))
                            mm(bank[1 + d][half, 0:P], w_[d][:, c, half], state[d]).then_inc(s["ws_made"], 1)
                    if n > 0:
                        fill(2)
                    for d in range(2):
                        c, r = chunk_of(n, d)
                        half = slice(r, r + CHUNK)
                        if n > 0:
                            pe.wait_ge(s["v_new"], 14 * h + (2 * (n - 1) + d + 1))
                        if n >= n_chunks // 2:
                            col = (2 * (c - QT) * CHUNK) + r
                            out = bank[3 + d][:, col:col + CHUNK]
                            mm(out, state[d], qd[d][:, c, half], True, False)
                            ins = mm(out, u_[d][half, c, :], qk[d][half, c, half], False, True)
                            if n == n_chunks - 1:
                                ins.then_inc(s["o_made"], 1)
                        if n < n_chunks - 1:
                            mm(bank[1 + d][:, P:2 * P], kd[d][half, c, :], u_[d][half, c, :]).then_inc(s["kv_made"], 1)
                    fill(2)

            project_head(0, 2 * KT, KT)
            with pe.Fori(0, HEADS - 1) as h:
                head(h, False)
            head(HEADS - 1, True)

            pe.wait_ge(s["head_free"], HEADS + 1)
            pe.wait_ge(s["heads_squared"], 1)
            for i in range(4):
                mm(bank[4 + i][:, :], ones[:, :], sq_gdn[:, i, :]).then_inc(s["heads_summed"], 1)
            n = 0

            def acc_bank():
                nonlocal n
                if n >= 4:
                    pe.wait_ge(s["rest_taken"], n - 3)
                n += 1
                return bank[(n - 1) % 4]

            for j in range(KT):
                acc = acc_bank()
                w = block_of(0, V0 + j, N_FIRST - 1)
                project_rows(acc, w, hc, SEQ).then_inc(s["rest_made"], 1)
                block_ends(V0 + j, N_FIRST - 1)
            for first in (U0, Z0):
                for j in range(KT):
                    acc = acc_bank()
                    w = block_of(0, first + j, N_FIRST - 1)
                    project(acc[:, 0:SEQ], w, H).then_inc(s["rest_made"], 1)
                    block_ends(first + j, N_FIRST - 1)

            def pair(first, j, moving):
                acc = acc_bank()
                for i in range(2):
                    w = block_of(0, first + 2 * j + i, N_FIRST - 1)
                    ins = project(acc[:, i * SEQ:(i + 1) * SEQ], w, moving[i])
                    block_ends(first + 2 * j + i, N_FIRST - 1)
                ins.then_inc(s["rest_made"], 1)

            for j in range(KT):
                pair(G0, j, (H, H))
            pe.wait_ge(s["v_normed"], 1)
            pe.wait_ge(s["head_landed"], 16 * (HEADS + 1))
            pe.wait_ge(s["tables_landed"], 64)
            for j in range(KT):
                if j >= 3:
                    pe.wait_ge(s["sgu_taken"], j - 2)
                for qt in range(QT):
                    out = bank[4 + j % 3][:, qt * P:(qt + 1) * P]
                    mm(out, v_rows[:, qt, j * P:(j + 1) * P], sgu_wT[:, j, :], True, False)
                    ins = mm(out, ones[0:1, :], one_row[0:1, 0, j * P:(j + 1) * P], False, True)
                ins.then_inc(s["sgu_mixed"], 1)
            pe.wait_ge(s["sgu_taken"], KT)
            for j in range(KT):
                pair(AB0, j, (y_gdn, y_sgu))
            pe.wait_ge(s["rest_taken"], n)
            for j in range(KT):
                if j >= 4:
                    pe.wait_ge(s["residual"], j - 3)
                w = block_of(0, O0 + j, N_FIRST - 1)
                project(bank[j % 4][:, 0:SEQ], w, merged).then_inc(s["rest_made"], 1)
                block_ends(O0 + j, N_FIRST - 1)

            def norm_sum(i):
                pe.wait_ge(s["norm_ready"], i + 1)
                column_sum(bank[4][:, 0:SEQ], HS).then_inc(s["norm_summed"], 1)

            def route(m, width, experts):
                pe.wait_ge(s[f"route_in{m}"], KT)
                pe.wait_ge(s["router_landed"], 16 * (m + 1))
                src = H if m == 0 else X
                for qt in range(QT):
                    out = bank[5][:, qt * width:(qt + 1) * width]
                    for k in range(KT):
                        mm(out, src[:, k, qt * P:(qt + 1) * P], router_w[m][:, k, :], k == 0, False)
                    at = D + (0, GROUPS1 + E1)[m]
                    ins = mm(out, ones[0:1, :], one_row[0:1, 0, at:at + width], False, True)
                ins.then_inc(s["logits_made"], 1)
                for qt in range(QT):
                    for k in range(KT):
                        i = qt * 2 + k // 4
                        ins = nc.tensor.transpose(bank[i][:, (k % 4) * P:(k % 4 + 1) * P], src[:, k, qt * P:(qt + 1) * P],
                                                  M("ident"))
                        if k % 4 == 3:
                            ins.then_inc(s["rows_turned"], 1)
                pe.wait_ge(s["kept"], m + 1)
                pe.wait_ge(s["attn_landed"], 16)
                mm(bank[6][:, 0:experts], earlier, keep[:, 0, 0:experts])
                mm(bank[6][:, experts:2 * experts], earlier, keep[:, 1, 0:experts], True, False)
                mm(bank[6][:, experts:2 * experts], ones[:, :], keep[:, 0, 0:experts], False, True)
                mm(bank[6][:, 2 * experts:3 * experts], ones[:, :], keep[:, 0, 0:experts], True, False)
                mm(bank[6][:, 2 * experts:3 * experts], ones[:, :], keep[:, 1, 0:experts], False, True
                   ).then_inc(s["placed"], 1)

            def make_lists(m, r):
                experts = SHAPES[m][0]
                pe.wait_ge(s["slots_marked"], QT * (2 * m + r + 1))
                for e in range(experts):
                    for qt in range(QT):
                        ins = mm(bank[7][:, 3 * e:3 * e + 3], onehot_slots[:, qt, e, :], facts[:, qt, e, :], qt == 0, qt == QT - 1)
                ins.then_inc(s["listed"], 1)

            def mixture_pass(m, r):
                experts, sub, g0 = SHAPES[m]
                slices, per = experts * sub, steps_per_turn(sub)
                e_per = per // sub
                ahead = 2 if sub == 1 else 1
                landed_, used = (landed, slots_used) if r == 0 else (landed2[m], used2)
                eb, sb_ = experts_before(m, r), slices_before(m, r)
                make_lists(m, r)

                def turn_x(t_, e):
                    pe.wait_ge(s["x_gathered"], e_per * t_ + (eb + e + 1))
                    if eb + e > 0:
                        pe.wait_ge(s["x_copied"], 2 * e_per * t_ + 2 * (eb + e))
                    for k in range(KT):
                        ins = nc.tensor.transpose(bank[3 + k // 4][:, (k % 4) * P:(k % 4 + 1) * P],
                                                  x_rows[e % NB][:, k * P:(k + 1) * P], M("ident"))
                    ins.then_inc(s["x_turned"], 1)

                def up(t_, i, half):
                    slot = (g0 + i) % RING
                    e = i // sub
                    if half == 0:
                        loads = (g0 + i) // RING + 1 if r == 0 else i // RING + 1
                        pe.wait_ge(landed_[slot], (16 * per // RING) * t_ + 16 * loads)
                        if i % sub == 0:
                            pe.wait_ge(s["x_copied"], 2 * e_per * t_ + 2 * (eb + e + 1))
                    w = ring[:, slot, 0:2 * KT * FS].rearrange("p (k f) -> p k f", k=KT)
                    for k in range(4 * half, 4 * half + 4):
                        ins = mm(bank[i % 2][:, :], x_cols[e % NB][:, k, :], w[:, k, :], k == 0, k == KT - 1)
                    if half == 1:
                        ins.then_inc(s["up_made"], 1)

                def turn_h(t_, i):
                    pe.wait_ge(s["hid_ready"], per * t_ + (sb_ + i + 1))
                    for f in range(2):
                        ins = nc.tensor.transpose(bank[2][:, f * P:(f + 1) * P], hid[i % 2][:, f * P:(f + 1) * P], M("ident"))
                    ins.then_inc(s["h_turned"], 1)

                def down(t_, i):
                    pe.wait_ge(s["h_copied"], per * t_ + (sb_ + i + 1))
                    e = i // sub
                    if i % sub == 0:
                        pe.wait_ge(s["y_ready"], 2 * e_per * t_ + 2 * (eb + e + 1))
                    slot = (g0 + i) % RING
                    w = ring[:, slot, 2 * KT * FS:].rearrange("p (f d) -> p f d", f=2)
                    for f in range(2):
                        for n_ in range(2):
                            ins = mm(bank[5 + n_][:, :], hid_T[i % 2][:, f, :], w[:, f, n_ * 512:(n_ + 1) * 512],
                                     i % sub == 0 and f == 0, i % sub == sub - 1 and f == 1)
                    ins.then_inc(used, 1)

                def step(t_, i, last_slice):
                    if not last_slice:
                        up(t_, i + 1, 0)
                    turn_h(t_, i)
                    if not last_slice:
                        up(t_, i + 1, 1)
                    if i % sub == 0 and (not (type(t_) is int) or i // sub + ahead < experts):
                        turn_x(t_, i // sub + ahead)
                    down(t_, i)

                turn_x(0, 0)
                up(0, 0, 0)
                up(0, 0, 1)
                if ahead == 2:
                    turn_x(0, 1)
                turns = (slices - 1) // per
                with pe.Fori(0, turns) as t_:
                    for i in range(per):
                        step(t_, i, False)
                for i in range(per * turns, slices):
                    step(0, i, i == slices - 1)

            def mixture(m):
                mixture_pass(m, 0)
                with pe.If(overflow(pe, m)):
                    mixture_pass(m, 1)
                n = E1 * E1_SUB
                if m == 0:
                    made_good(pe, 0, [(s["listed"], 1, 1), (s["x_turned"], E1, E1), (s["up_made"], n, n),
                                      (s["h_turned"], n, n), (used2, 0, n),
                                      (s["x_copied"], 2 * E1, 2 * E1), (s["y_ready"], 2 * E1 + 2, 2 * E1)])
                pe.wait_ge(s["y_summed"], m + 1)
                for j in range(KT):
                    for qt in range(QT):
                        at = (j % 2) * SEQ + qt * P
                        ins = nc.tensor.transpose(bank[4 + j // 2][:, at:at + P], y_sum[:, qt, j * P:(j + 1) * P], M("ident"))
                ins.then_inc(s["y_turned"], 1)

            norm_sum(0)
            route(0, GROUPS1 + E1, E1)
            pe.sem_inc(s["y_ready"], 2)
            mixture(0)
            norm_sum(1)

            pe.wait_ge(s["x3_ready"], 1)
            n2 = 0
            for j in range(O20):
                if n2 >= 4:
                    pe.wait_ge(s["qkv2_taken"], n2 - 3)
                acc = bank[n2 % 4]
                n2 += 1
                w = block_of(SECOND_G, j, N_SECOND - 1)
                if VS0 <= j < QD0 or j >= VD0:
                    ins = project_rows(acc, w, X, 0)
                else:
                    ins = project(acc[:, 0:SEQ], w, X)
                ins.then_inc(s["qkv2_made"], 1)
                block_ends(j, N_SECOND - 1)
            pe.wait_ge(s["qkv2_taken"], O20)
            pe.wait_ge(s["attn_landed"], 16)
            def sb_scores(a):
                rows = slice(DH2 * (a % 2), DH2 * (a % 2) + DH2)
                if a >= 2:
                    pe.wait_ge(s["sb_exponent"], a - 1)
                for kt in range(QT):
                    ins = mm(bank[Z_BANKS[a % 2]][:, kt * SEQ:(kt + 1) * SEQ], ks[rows, a // 2, kt * P:(kt + 1) * P], qs[rows, a // 2, :])
                ins.then_inc(s["scored"], 1)

            def sb_between(a):
                pe.wait_ge(s["sb_logs"], a + 1)
                lm = sc[2 + a % 2]
                out = bank[2]
                if a >= 1:
                    pe.wait_ge(s["sb_exponent"], a)
                mm(out[:, SEQ:2 * SEQ], after, lm[:, 1, :])
                mm(out[:, 0:SEQ], after, lm[:, 0, :], True, False)
                mm(out[:, 0:SEQ], ones[:, :], lm[:, 1, :], False, True).then_inc(s["sb_between"], 1)

            def sb_values(a):
                rows = slice(DH2 * (a % 2), DH2 * (a % 2) + DH2)
                pe.wait_ge(s["sb_weights"], a + 1)
                if a >= 2 and a % 2 == 0:
                    pe.wait_ge(s["o_taken"], a - 1)
                for kt in range(QT):
                    ins = mm(bank[4][rows, 0:SEQ], vs[:, kt, a * DH2:(a + 1) * DH2], sc[4 + a % 2][:, kt, :],
                             kt == 0, kt == QT - 1)
                ins.then_inc(s["valued"], 1)

            pe.wait_ge(s["bias_landed"], 32)

            def dl_scores(a):
                rows = slice(DH2 * (a % 2), DH2 * (a % 2) + DH2)
                if a >= 2:
                    pe.wait_ge(s["dl_exped"], 2 * (a - 1))
                for qt in range(QT):
                    out = bank[SCORE_BANKS[a % 2]][:, qt * SEQ:(qt + 1) * SEQ]
                    mm(out, qd2[rows, a // 2, qt * P:(qt + 1) * P], kd2[rows, a // 2, :], True, False)
                    ins = mm(out, flip, bias2[:, a, qt, :], False, True)
                ins.then_inc(s["scored"], 1)

            def dl_turn(a):
                pe.wait_ge(s["dl_probs"], a + 1)
                if a >= 1:
                    pe.wait_ge(s["dl_turned_copied"], a)
                for kt in range(QT):
                    for qt in range(QT):
                        ins = nc.tensor.transpose(bank[3][:, kt * SEQ + qt * P:kt * SEQ + (qt + 1) * P],
                                                  sd[2 + a % 2][:, qt, kt * P:(kt + 1) * P], M("ident"))
                ins.then_inc(s["dl_turned"], 1)

            def dl_values(a):
                rows = slice(DH2 * (a % 2), DH2 * (a % 2) + DH2)
                pe.wait_ge(s["dl_turned_copied"], a + 1)
                if a >= 2 and a % 2 == 0:
                    pe.wait_ge(s["o_taken"], a)
                for kt in range(QT):
                    ins = mm(bank[5][rows, 0:SEQ], vd2[:, kt, a * DH2:(a + 1) * DH2], sd[4 + a % 2][:, kt, :],
                             kt == 0, kt == QT - 1)
                ins.then_inc(s["valued"], 1)

            for a in range(-1, H2 + 2):
                if 1 <= a <= H2:
                    sb_between(a - 1)
                if a >= 2:
                    sb_values(a - 2)
                    dl_values(a - 2)
                if a + 1 < H2:
                    sb_scores(a + 1)
                    dl_scores(a + 1)
                if 1 <= a <= H2:
                    dl_turn(a - 1)
            pe.wait_ge(s["heads_squared"], 2)
            for i in range(4):
                mm(bank[i][:, :], M("same"), sq_att[:, i, :]).then_inc(s["heads_summed"], 1)
            pe.wait_ge(s["att_normed"], 1)
            for j in range(KT):
                if j >= 4:
                    pe.wait_ge(s["residual"], 2 * KT + j - 3)
                w = block_of(SECOND_G, O20 + j, N_SECOND - 1)
                project(bank[j % 4][:, 0:SEQ], w, o_att).then_inc(s["out2_made"], 1)
                block_ends(O20 + j, N_SECOND - 1)

            def layer_norm_sums(i):
                pe.wait_ge(s["residual"], KT * (i + 3))
                column_sum(bank[4][:, 0:SEQ], X).then_inc(s["ln_mean"], 1)
                pe.wait_ge(s["ln_sq"], i + 1)
                column_sum(bank[5][:, 0:SEQ], HS).then_inc(s["ln_var"], 1)

            layer_norm_sums(0)
            route(1, E2, E2)
            mixture(1)
            layer_norm_sums(1)

        @block.scalar
        def _(act):
            link = Chain(act, s["act_chain"])

            def act_fn(out, in_, func, **kw):
                return nc.scalar.activation(out, in_, func, **kw)

            act.wait_ge(s["vec_landed"], 16)
            act_fn(cs[:, :, :].rearrange("p a b -> p (a b)"), V("cond"), ACT.Silu).then_inc(s["cond_ready"], 1)
            act.wait_ge(s["xc_landed"], 16)
            act_fn(hc[:, :, :], xc[:, :, :], ACT.Square).then_inc(s["xc_squared"], 1)

            def rsqrt(out, in_, scale, eps):
                link(act_fn(out, in_, ACT.Ln, scale=scale, bias=eps_ap[eps]))
                return act_fn(out, out, ACT.Exp, scale=-0.5)

            act.wait_ge(s["xc_summed"], 1)
            act.wait_ge(s["constants_set"], 4)
            rsqrt(area(0, 512), bank[1][:, :], 1.0 / D, EPS).then_inc(s["xc_rnorm"], 1)
            for i in range(6 * KT // ADA_BLOCKS):
                act.wait_ge(s["ada_made"], i + 1)
                n_ = ADA_BLOCKS * P
                act_fn(ada_rows[0:2, i * n_:(i + 1) * n_], bank[3 + i % 2][0:2, 0:n_], ACT.Copy).then_inc(s["ada_copied"], 1)
            act.wait_ge(s["bias_made"], 1)
            act_fn(bias_row, bank[5][0:H2, :], ACT.Copy).then_inc(s["bias_copied"], 1)
            act.wait_ge(s["a_in"], 1)
            act_fn(gd["beta"][:, :, :], gates_in[:, :, 0:DH], ACT.Sigmoid).then_inc(s["beta_ready"], 1)
            link(act_fn(gd["t"][:, :, :], gates_in[:, :, DH:2 * DH], ACT.Abs))
            link(act_fn(gd["t"][:, :, :], gd["t"][:, :, :], ACT.Exp, scale=-1.0))
            act_fn(gd["t"][:, :, :], gd["t"][:, :, :], ACT.Ln, bias=eps_ap[1.0]).then_inc(s["soft_ready"], 1)
            act_fn(gd["kb"][:, 0, :], V("a_log"), ACT.Exp).then_inc(s["soft_ready"], 1)
            act.wait_ge(s["cum_ready"], 1)
            act_fn(gd["t"][:, :, :], gd["G"][:, :, :], ACT.Exp).then_inc(s["cum_exp"], 1)
            act_fn(gd["kd"][:, :, :], gd["kd"][:, :, :], ACT.Exp).then_inc(s["cum_exp"], 1)

            act.wait_ge(s["pads_zeroed"], 3)
            def pad_rows(h, j):
                act.wait_ge(s["projected"], 3 * h + (j + 1))
                act_fn(pad[j][:, :, 2:2 + SEQ], bank[PROJECTED[j]][:, :].rearrange("p (a b) -> p a b", a=2), ACT.Copy
                       ).then_inc(s["padded"], 1)

            def activate(h, j):
                act.wait_ge(s["conved"], 3 * h + (j + 1))
                act_fn(conv[j], conv[j], ACT.Silu).then_inc(s["activated"], 1)
                if j < 2:
                    act.wait_ge(s["activated"], 3 * h + (j + 1))
                    act_fn(norms[j], conv[j], ACT.Square).then_inc(s["squared"], 1)

            def take_projected(h):
                pad_rows(h, 0)
                pad_rows(h, 1)
                activate(h, 0)
                pad_rows(h, 2)
                activate(h, 1)

            def head(h, last):
                n2 = [norms[j].rearrange("p a b -> p (a b)") for j in range(2)]
                for j in range(2):
                    act.wait_ge(s["sq_summed"], 2 * h + (j + 1))
                    link(act_fn(n2[j], bank[3 + j][:, :], ACT.Ln, bias=eps_ap[EPS]))
                for j in (1, 0):
                    act_fn(n2[j], n2[j], ACT.Exp, scale=-0.5).then_inc(s["norms_ready"], 1)
                for d in range(2):
                    act.wait_ge(s["g_diffs"], 2 * h + (d + 1))
                    act_fn(et[d], et[d], ACT.Exp).then_inc(s["decays"], 1)
                for d in range(2):
                    act_fn(tmp[d].rearrange("p a b -> p (a b)"), bank[1 + d][:, :], ACT.Exp).then_inc(s["exp_g"], 1)
                activate(h, 2)
                for d in range(2):
                    act.wait_ge(s["inverse_turned"], 2 * h + (d + 1))
                    act_fn(D_[d].rearrange("p a b -> p (a b)"), bank[1 + d][:, :], ACT.Copy).then_inc(s["d_copied"], 1)
                for k in range(1, LEVELS):
                    for d in range(2):
                        act.wait_ge(s["y_made"], 10 * h + (2 * (k - 1) + d + 1))
                        if k > 1:
                            act.wait_ge(s["ey_made"], 10 * h + (2 * (k - 2) + d + 1))
                        act_fn(Y_[d].rearrange("p a b -> p (a b)"), bank[3 + d][:, :], ACT.Copy).then_inc(s["y_copied"], 1)
                for i in range(4):
                    act.wait_ge(s["uw_made"], 4 * h + (i + 1))
                    dst = (u_ if i < 2 else w_)[i % 2]
                    act_fn(dst.rearrange("p a b -> p (a b)"), bank[3 + i][:, :], ACT.Copy).then_inc(s["uw_copied"], 1)
                if not last:
                    take_projected(h + 1)
                act.wait_ge(s["o_made"], 2 * h + 1)
                act_fn(tmp[0].rearrange("p a b -> p (a b)")[:, 0:SEQ], bank[3][:, 0:SEQ], ACT.Copy).then_inc(s["o_copied"], 1)

            take_projected(0)
            with act.Fori(0, HEADS - 1) as h:
                link.enter(h, 2)
                head(h, False)
            link.leave(HEADS - 1)
            head(HEADS - 1, True)

            for i in range(4):
                act.wait_ge(s["heads_summed"], i + 1)
                rsqrt(r_gdn[:, i, :], bank[4 + i][:, :], 1.0 / P, EPS).then_inc(s["heads_rnorm"], 1)
            for j in range(KT):
                act.wait_ge(s["rest_made"], j + 1)
                act_fn(v_rows[:, :, j * P:(j + 1) * P], bank[j % 4][:, 0:SEQ].rearrange("p (a b) -> p a b", a=QT),
                       ACT.Gelu_apprx_tanh).then_inc(s["rest_taken"], 1)
            for j in range(KT):
                act.wait_ge(s["rest_made"], KT + j + 1)
                act_fn(u_cols[:, j, :], bank[j % 4][:, 0:SEQ], ACT.Gelu_apprx_tanh).then_inc(s["rest_taken"], 1)
            for j in range(KT):
                act.wait_ge(s["rest_made"], 2 * KT + j + 1)
                act_fn(z_cols[:, j, :], bank[j % 4][:, 0:SEQ], ACT.Silu).then_inc(s["rest_taken"], 1)
            for j in range(KT):
                act.wait_ge(s["rest_made"], 3 * KT + j + 1)
                act_fn(gate_cols[:, j, :], bank[j % 4][:, :], ACT.Sigmoid).then_inc(s["rest_taken"], 1)
            act.wait_ge(s["v_stats"], 1)
            rsqrt(bn_r[:, :], bn_mv[:, :, 1], 1.0, EPS).then_inc(s["v_rstd"], 1)

            def norm(i, eps):
                act.wait_ge(s["residual"], KT * (i + 1))
                act_fn(HS, X, ACT.Square).then_inc(s["norm_ready"], 1)
                act.wait_ge(s["norm_summed"], i + 1)
                rsqrt(norm_r, bank[4][:, 0:SEQ], 1.0 / D, eps).then_inc(s["rnorm"], 1)

            def route(m, experts):
                act.wait_ge(s["route_exp_in"], 2 * m + 1)
                if m == 0:
                    n_ = QT * GROUPS1
                    act_fn(rt[1][:, 0:n_], rt[1][:, 0:n_], ACT.Exp).then_inc(s["route_exp"], 1)
                    act.wait_ge(s["route_exp_in"], 2)
                    act_fn(rt[5][:, :], rt[5][:, :], ACT.Exp).then_inc(s["route_exp"], 1)
                else:
                    n_ = QT * E2
                    act_fn(rt[1][:, 0:n_], rt[1][:, 0:n_], ACT.Exp).then_inc(s["route_exp"], 1)
                for i in range(4):
                    act.wait_ge(s["rows_turned"], 4 * m + i + 1)
                    act_fn(own_rows[:, i // 2, (i % 2) * 512:(i % 2 + 1) * 512], bank[i][:, :], ACT.Copy
                           ).then_inc(s["rows_copied"], 1)

            def mixture_pass(m, r):
                experts, sub, _ = SHAPES[m]
                slices, per = experts * sub, steps_per_turn(sub)
                e_per = per // sub
                ahead = 2 if sub == 1 else 1
                eb, sb_ = experts_before(m, r), slices_before(m, r)

                def silu(t_, i):
                    act.wait_ge(s["up_made"], per * t_ + (sb_ + i + 1))
                    act_fn(act_h[i % 2], bank[i % 2][:, 0:FS], ACT.Silu).then_inc(s["silu_made"], 1)

                def copy_h(t_, i):
                    act.wait_ge(s["h_turned"], per * t_ + (sb_ + i + 1))
                    act_fn(hid_T[i % 2].rearrange("p a b -> p (a b)"), bank[2][:, 0:FS], ACT.Copy
                           ).then_inc(s["h_copied"], 1)

                def copy_x(t_, e):
                    act.wait_ge(s["x_turned"], e_per * t_ + (eb + e + 1))
                    act_fn(x_cols[e % NB][:, 0:4, :].rearrange("p a b -> p (a b)"), bank[3][:, :], ACT.Copy
                           ).then_inc(s["x_copied"], 1)

                def copy_y(t_, i):
                    e = i // sub
                    if r == 0:
                        act.wait_ge(slots_used, per * t_ + (i + 1 + (MOE1_G, MOE2_G)[m]))
                    else:
                        act.wait_ge(used2, per * t_ + (i + 1 + m * E1 * E1_SUB))
                    act.wait_ge(s["y_free"], e_per * t_ + (eb + e + 1))
                    act_fn(y_rows[e % NB][:, 0:512], bank[5][:, :], ACT.Copy).then_inc(s["y_ready"], 1)

                def step(t_, i, last_slice):
                    copy_h(t_, i)
                    if not last_slice:
                        silu(t_, i + 1)
                    if i % sub == 0 and (not (type(t_) is int) or i // sub + ahead < experts):
                        copy_x(t_, i // sub + ahead)
                    if i % sub == sub - 1:
                        copy_y(t_, i)

                copy_x(0, 0)
                silu(0, 0)
                if ahead == 2:
                    copy_x(0, 1)
                turns = (slices - 1) // per
                with act.Fori(0, turns) as t_:
                    for i in range(per):
                        step(t_, i, False)
                for i in range(per * turns, slices):
                    step(0, i, i == slices - 1)

            def mixture(m):
                mixture_pass(m, 0)
                with act.If(overflow(act, m)):
                    mixture_pass(m, 1)
                n = E1 * E1_SUB
                if m == 0:
                    made_good(act, 0, [(s["silu_made"], n, n), (s["h_copied"], n, n)])

            norm(0, EPS)
            route(0, E1)
            mixture(0)
            norm(1, EPS)
            for j in range(O20):
                act.wait_ge(s["qkv2_made"], j + 1)
                acc = bank[j % 4]
                part, i = divmod(j, 4)
                if part in (2, 5):
                    dst = (vs if part == 2 else vd2)[:, :, i * P:(i + 1) * P]
                    act_fn(dst, acc[:, 0:SEQ].rearrange("p (a b) -> p a b", a=QT), ACT.Copy).then_inc(s["qkv2_taken"], 1)
                else:
                    dst = {0: qs, 1: ks, 3: qd2, 4: kd2}[part][:, i, :]
                    act_fn(dst, acc[:, 0:SEQ], ACT.Copy, scale=DH2 ** -0.5 if part in (0, 3) else 1.0
                           ).then_inc(s["qkv2_taken"], 1)
            def sb_exp_abs(a):
                act.wait_ge(s["scored"], 2 * a + 1)
                b = sc[a % 2].rearrange("p a b -> p (a b)")
                if a >= 2:
                    act.wait_ge(s["sb_exponent"], a - 1)
                link(act_fn(b, bank[Z_BANKS[a % 2]][:, :], ACT.Abs))
                link(act_fn(b, b, ACT.Exp, scale=-1.0))

            def sb_soft(a):
                b = sc[a % 2].rearrange("p a b -> p (a b)")
                act_fn(b, b, ACT.Ln, bias=eps_ap[1.0]).then_inc(s["sb_soft"], 1)

            def sb_exp(a):
                act.wait_ge(s["sb_exponent"], a + 1)
                act_fn(sc[4 + a % 2], sc[4 + a % 2], ACT.Exp).then_inc(s["sb_exped"], 1)

            def dl_exp(a):
                act.wait_ge(s["dl_shifted"], a + 1)
                if a >= 2:
                    act.wait_ge(s["dl_probs"], a - 1)
                for qt in range(QT):
                    act_fn(sd[a % 2][:, qt, :], bank[SCORE_BANKS[a % 2]][:, qt * SEQ:(qt + 1) * SEQ], ACT.Exp,
                           bias=am[:, a % 2, qt:qt + 1]).then_inc(s["dl_exped"], 1)

            def dl_copy(a):
                act.wait_ge(s["dl_turned"], a + 1)
                if a >= 2:
                    act.wait_ge(s["valued"], 2 * a - 2)
                act_fn(sd[4 + a % 2].rearrange("p a b -> p (a b)"), bank[3][:, :], ACT.Copy
                       ).then_inc(s["dl_turned_copied"], 1)

            for a in range(H2 + 1):
                if a < H2:
                    sb_exp_abs(a)
                    dl_exp(a)
                if a >= 1:
                    sb_exp(a - 1)
                if a < H2:
                    sb_soft(a)
                if a >= 1:
                    dl_copy(a - 1)
            for i in range(4):
                act.wait_ge(s["heads_summed"], i + 5)
                rsqrt(r_att[:, i, :], bank[i][:, :], 1.0 / DH2, EPS).then_inc(s["heads_rnorm"], 1)

            def layer_norm(i):
                act.wait_ge(s["ln_mean"], i + 1)
                act_fn(norm_m, bank[4][:, 0:SEQ], ACT.Copy, scale=1.0 / D).then_inc(s["ln_mean_copied"], 1)
                act.wait_ge(s["ln_centred"], i + 1)
                act_fn(HS, X, ACT.Square).then_inc(s["ln_sq"], 1)
                act.wait_ge(s["ln_var"], i + 1)
                rsqrt(norm_r, bank[5][:, 0:SEQ], 1.0 / D, LN_EPS).then_inc(s["ln_rnorm"], 1)

            layer_norm(0)
            route(1, E2)
            mixture(1)
            layer_norm(1)

        @block.vector
        def _(dve):
            link = Chain(dve, s["dve_chain"])
            tt_, ts_, stt = nc.vector.tensor_tensor, nc.vector.tensor_scalar, nc.vector.scalar_tensor_tensor
            red, cp = nc.vector.tensor_reduce, nc.vector.tensor_copy

            nc.vector.memset(ones[:, :], 1.0).then_inc(s["constants_set"], 1)
            for value in (EPS, LN_EPS, 1.0):
                nc.vector.memset(eps_ap[value], value).then_inc(s["constants_set"], 1)
            dve.wait_ge(s["vec_landed"], 16)
            dve.wait_ge(s["xc_rnorm"], 1)
            link(tt_(hc[:, :, :], xc[:, :, :], times(area(0, 512), KT), ALU.mult))
            dve.wait_ge(s["mod_made"], 1)
            link(tt_(mod[:, :, :], bank[2][:, 0:12 * KT].rearrange("p (a b) -> p a b", b=2), over(V("ada_b"), 2), ALU.add))
            link(stt(mixs[:, :, :], mod[:, KT:2 * KT, :], 1.0, over(V("norm_mix_g"), 2), ALU.add, ALU.mult))
            link(stt(ffns[:, :], mod[:, 4 * KT:5 * KT, 0], 1.0, V("norm_ffn_g"), ALU.add, ALU.mult))
            for k in range(KT):
                for who, cols in ((1, slice(0, SEQ)), (0, slice(SEQ, TOK))):
                    ins = ts_(hc[:, k, cols], hc[:, k, cols], mixs[:, k, who:who + 1], mod[:, k, who:who + 1],
                              ALU.mult, ALU.add)
                ins.then_inc(s["modulated"], 1)
            for j in range(3):
                nc.vector.memset(pad[j], 0.0).then_inc(s["pads_zeroed"], 1)
            dve.wait_ge(s["ba_made"], 1)
            ba = bank[3][:, 0:TT * 2 * DH].rearrange("p (a b) -> p a b", a=TT)
            link(cp(gates_in[:, :, 0:DH], ba[:, :, 0:DH]))
            tt_(gates_in[:, :, DH:2 * DH], ba[:, :, DH:2 * DH], times(V("dt_bias"), TT), ALU.add).then_inc(s["a_in"], 1)
            dve.wait_ge(s["a_in"], 1)
            dve.wait_ge(s["soft_ready"], 2)
            link(stt(gd["g"][:, :, :], gates_in[:, :, DH:2 * DH], 0.0, gd["t"][:, :, :], ALU.max, ALU.add))
            stt(gd["g"][:, :, :], gd["g"][:, :, :], -1.0, times(gd["kb"][:, 0, :], TT), ALU.mult, ALU.mult
                ).then_inc(s["g_raw"], 1)
            dve.wait_ge(s["cum_made"], 1)
            link(cp(gd["G"][:, :, 0:HEADS], bank[1][:, 0:32].rearrange("p (a b) -> p a b", a=TT)))
            link(cp(gd["G"][:, :, HEADS:DH], bank[1][:, 32:64].rearrange("p (a b) -> p a b", a=TT)))
            tt_(gd["kd"][:, :, :], bank[1][:, 64:128].rearrange("p (a b) -> p a b", a=TT), gd["G"][:, :, :], ALU.subtract
                ).then_inc(s["cum_ready"], 1)
            dve.wait_ge(s["cum_exp"], 2)
            dve.wait_ge(s["beta_ready"], 1)
            link(tt_(gd["kb"][:, :, :], gd["beta"][:, :, :], gd["t"][:, :, :], ALU.mult))
            nc.vector.memset(bn_r[:, :], 0.0).then_inc(s["g_ready"], 1)
            dve.wait_ge(s["g_ready"], 1)
            dve.wait_ge(s["bias_copied"], 1)

            def conv_taps(h, j, first, end):
                if first == 0:
                    dve.wait_ge(s["padded"], 3 * h + (j + 1))
                c3 = conv[j].rearrange("p a b -> p (a b)").rearrange("p (a b) -> p a b", a=2)
                for i in range(first, end):
                    wgt = V("conv_w")[:, bass.ds(h * (3 * CONV) + (j * CONV + i), 1)]
                    src = pad[j][:, :, i:i + SEQ]
                    if i == 0:
                        link(ts_(c3, src, wgt, None, ALU.mult))
                    elif i < CONV - 1:
                        link(stt(c3, src, wgt, c3, ALU.mult, ALU.add))
                    else:
                        stt(c3, src, wgt, c3, ALU.mult, ALU.add).then_inc(s["conved"], 1)

            def head(h, last):
                for d in range(2):
                    dve.wait_ge(s["gram"], 8 * h + (d + 1))
                    for a in range(TT):
                        ins = ts_(et[d][:, a, :], bank[1 + d][:, a * P:(a + 1) * P],
                                  gd["G"][:, a, bass.ds(h + HEADS * d, 1)], 0.0, ALU.subtract, ALU.min)
                    ins.then_inc(s["g_diffs"], 1)
                dve.wait_ge(s["norms_ready"], 2 * h + 1)
                tt_(conv[1], conv[1], norms[1], ALU.mult).then_inc(s["normed"], 1)
                dve.wait_ge(s["norms_ready"], 2 * h + 2)
                stt(conv[0].rearrange("p a b -> p (a b)"), conv[0].rearrange("p a b -> p (a b)"), float(P) ** -0.5,
                    norms[0].rearrange("p a b -> p (a b)"), ALU.mult, ALU.mult).then_inc(s["normed"], 1)
                dve.wait_ge(s["normed"], 2 * h + 2)
                for d in range(2):
                    dve.wait_ge(s["decays"], 2 * h + (d + 1))
                    dve.wait_ge(s["gram"], 8 * h + 6)
                    e2 = et[d].rearrange("p a b -> p (a b)")
                    u2 = up[d].rearrange("p a b -> p (a b)")
                    link(tt_(u2, bank[7][:, :], e2, ALU.mult))
                    tt_(u2, bank[3 + d][:, :], u2, ALU.mult).then_inc(s["couplings"], 1)
                for d in range(2):
                    dve.wait_ge(s["couplings"], 2 * h + (d + 1))
                    link(tt_(E_[d], up[d], times(M(f"level0_{'fb'[d]}"), TT), ALU.mult))
                    tt_(E_[d], times(M("ident"), TT), E_[d], ALU.subtract).then_inc(s["first_inverse"], 1)
                for src, made, of, dsts in ((gd["kb"], 5, bank[5], kb), (gd["kd"], 5, bank[5], kd), (gd["beta"], 8, bank[6], vb)):
                    dve.wait_ge(s["gram"], 8 * h + made)
                    for d in range(2):
                        tt_(dsts[d], of[:, :].rearrange("p (a b) -> p a b", a=TT),
                            src[:, :, bass.ds(h + HEADS * d, 1)].broadcast_to([P, TT, P]), ALU.mult
                            ).then_inc(s["rows_scaled"], 1)
                dve.wait_ge(s["gram"], 8 * h + 7)
                for d in range(2):
                    tt_(qk[d].rearrange("p a b -> p (a b)"), bank[0][:, :], et[d].rearrange("p a b -> p (a b)"), ALU.mult
                        ).then_inc(s["rows_scaled"], 1)
                for k in range(1, LEVELS):
                    for d in range(2):
                        if k < LEVELS - 1:
                            dve.wait_ge(s["dy_made"], 8 * h + (2 * (k - 1) + d + 1))
                            dd = D_[d].rearrange("p a b -> p (a b)")
                            if k == 1:
                                dve.wait_ge(s["d_copied"], 2 * h + (d + 1))
                            else:
                                dve.wait_ge(s["d_updated"], 8 * h + (2 * (k - 2) + d + 1))
                            tt_(dd, dd, bank[5 + d][:, :], ALU.subtract).then_inc(s["d_updated"], 1)
                        dve.wait_ge(s["ey_made"], 10 * h + (2 * (k - 1) + d + 1))
                        if k == 1:
                            dve.wait_ge(s["first_inverse"], 2 * h + (d + 1))
                        else:
                            dve.wait_ge(s["e_updated"], 10 * h + (2 * (k - 2) + d + 1))
                        ee = E_[d].rearrange("p a b -> p (a b)")
                        tt_(ee, ee, bank[1 + d][:, :], ALU.subtract).then_inc(s["e_updated"], 1)
                n_chunks = TOK // CHUNK
                at = 0

                def fill(n):
                    nonlocal at
                    for _ in range(0 if last or n < 3 else 1 if n < 5 else 2):
                        if at < 2 * CONV:
                            conv_taps(h + 1, at // CONV, at % CONV, at % CONV + 1)
                            at += 1

                for n in range(n_chunks):
                    for d in range(2):
                        c, r = chunk_of(n, d)
                        half = slice(r, r + CHUNK)
                        if n > 0:
                            dve.wait_ge(s["ws_made"], 14 * h + (2 * (n - 1) + d + 1))
                            dve.wait_ge(s["uw_copied"], 4 * h + 4)
                            tt_(u_[d][half, c, :], u_[d][half, c, :], bank[1 + d][half, 0:P], ALU.subtract
                                ).then_inc(s["v_new"], 1)
                    fill(n)
                    for d in range(2):
                        c, r = chunk_of(n, d)
                        if n == n_chunks - 1:
                            continue
                        dve.wait_ge(s["kv_made"], 14 * h + (2 * n + d + 1))
                        if n == 0:
                            cp(state[d], bank[1 + d][:, P:2 * P]).then_inc(s["stepped"], 1)
                        else:
                            dve.wait_ge(s["stepped"], 14 * h + (2 * (n - 1) + d + 1))
                            end = r + CHUNK - 1 if d == 0 else r
                            stt(state[d], state[d], tmp[d][:, c, end:end + 1], bank[1 + d][:, P:2 * P], ALU.mult, ALU.add
                                ).then_inc(s["stepped"], 1)
                    fill(n)
                dve.wait_ge(s["o_made"], 2 * h + 2)
                dve.wait_ge(s["o_copied"], h + 1)
                tt_(o_heads[:, bass.ds(h, 1), :].rearrange("p a b -> p (a b)"),
                    tmp[0].rearrange("p a b -> p (a b)")[:, 0:SEQ], bank[4][:, 0:SEQ], ALU.add).then_inc(s["head_free"], 1)
                if not last:
                    conv_taps(h + 1, 2, 0, CONV)

            conv_taps(0, 0, 0, CONV)
            conv_taps(0, 1, 0, CONV)
            nc.vector.memset(state[0], 0.0).then_inc(s["head_free"], 1)
            dve.wait_ge(s["head_free"], 1)
            conv_taps(0, 2, 0, CONV)
            with dve.Fori(0, HEADS - 1) as h:
                link.enter(h, 3 * (CONV - 1) + 4)
                head(h, False)
            link.leave(HEADS - 1)
            head(HEADS - 1, True)

            dve.wait_ge(s["head_free"], HEADS + 1)
            oh = o_heads[:, :, :].rearrange("p a b -> p (a b)")
            tt_(sq_gdn.rearrange("p a b -> p (a b)"), oh, oh, ALU.mult).then_inc(s["heads_squared"], 1)
            dve.wait_ge(s["heads_rnorm"], 4)
            yg = y_gdn.rearrange("p a b -> p (a b)")
            stt(yg, oh, V("gdn_norm_g"), r_gdn.rearrange("p a b -> p (a b)"), ALU.mult, ALU.mult).then_inc(s["gdn_normed"], 1)
            dve.wait_ge(s["rest_taken"], KT)
            for qt in range(QT):
                for i in range(2):
                    link(nc.vector.bn_stats(bn[:, qt, i, :], v_rows[:, qt, i * 512:(i + 1) * 512]))
                ins = nc.vector.bn_aggr(bn_mv[:, qt, :], bn[:, qt, :, :].rearrange("p a b -> p (a b)"))
                if qt < QT - 1:
                    link(ins)
            ins.then_inc(s["v_stats"], 1)
            dve.wait_ge(s["rest_taken"], 3 * KT)
            dve.wait_ge(s["gdn_normed"], 1)
            link(tt_(yg, yg, z_cols.rearrange("p a b -> p (a b)"), ALU.mult))
            dve.wait_ge(s["v_rstd"], 1)
            dve.wait_ge(s["head_landed"], 16 * (HEADS + 1))
            for qt in range(QT):
                link(ts_(v_rows[:, qt, :], v_rows[:, qt, :], bn_mv[:, qt, 0:1], bn_r[:, qt:qt + 1], ALU.subtract, ALU.mult))
            link(tt_(v_rows, v_rows, times(ln_rows[:, 0, :], QT), ALU.mult))
            tt_(v_rows, v_rows, times(ln_rows[:, 1, :], QT), ALU.add).then_inc(s["v_normed"], 1)
            for j in range(KT):
                dve.wait_ge(s["sgu_mixed"], j + 1)
                tt_(y_sgu[:, j, :], bank[4 + j % 3][:, 0:SEQ], u_cols[:, j, :], ALU.mult).then_inc(s["sgu_taken"], 1)
            for j in range(KT):
                dve.wait_ge(s["rest_made"], 4 * KT + j + 1)
                dve.wait_ge(s["rest_taken"], 4 * KT + j)
                link(tt_(gate_cols[:, j, :], gate_cols[:, j, :], bank[j % 4][:, :], ALU.mult))
                tt_(merged[:, j, :], gate_cols[:, j, 0:SEQ], gate_cols[:, j, SEQ:2 * SEQ], ALU.add
                    ).then_inc(s["rest_taken"], 1)
            for j in range(KT):
                dve.wait_ge(s["rest_made"], 5 * KT + j + 1)
                ins = stt(X[:, j, :], bank[j % 4][:, 0:SEQ], mod[:, 2 * KT + j, 0:1], X[:, j, :], ALU.mult, ALU.add)
                ins.then_inc(s["residual"], 1)
            dve.wait_ge(s["rnorm"], 1)
            link(tt_(H, X, times(norm_r, KT), ALU.mult))
            for k in range(KT):
                ts_(H[:, k, :], H[:, k, :], ffns[:, k:k + 1], mod[:, 3 * KT + k, 0:1], ALU.mult, ALU.add
                    ).then_inc(s["route_in0"], 1)

            falling, pick_m = rt[7][:, 0:E1], rs[7]

            def first_largest(out, values, largest, c):
                rows = out.shape[1]
                link(tt_(out, values, over(largest, c), ALU.is_equal))
                link(tt_(out, out, times(falling[:, 0:c], rows), ALU.mult))
                link(red(pick_m[:, 0:rows], out, AX_X, ALU.max))
                return tt_(out, out, over(pick_m[:, 0:rows], c), ALU.is_equal)

            def make_falling():
                dve.wait_ge(s["attn_landed"], 16)
                link(ts_(falling, slot_numbers[:, 0:E1], -1.0, float(P), ALU.mult, ALU.add))

            def place_tokens(m, kept, gates):
                experts = SHAPES[m][0]
                first = rt[8][:, 0:QT * experts].rearrange("p (a b) -> p a b", a=QT)
                prod = rt[9][:, 0:QT * experts].rearrange("p (a b) -> p a b", a=QT)
                second_ = second[:, :, 0:experts]
                top = rs[6][:, 0:QT]
                link(red(choice_gates[:, 0, :], gates, AX_X, ALU.max))
                link(first_largest(first, gates, choice_gates[:, 0, :], experts))
                link(tt_(second_, kept, first, ALU.subtract))
                link(tt_(prod, second_, gates, ALU.mult))
                link(red(choice_gates[:, 1, :], prod, AX_X, ALU.add))
                link(cp(facts[:, :, 0:experts, 0], over(V("token"), experts)))
                link(cp(facts[:, :, 0:experts, 1], second_))
                link(nc.vector.memset(facts[:, :, 0:experts, 2], 1.0))
                dve.wait_ge(s["placed"], m + 1)
                place = position[:, :, 0:experts]
                link(ts_(prod, kept, -1.0, -float(SKIP), ALU.add, ALU.mult))
                link(tt_(place, bank[6][:, 0:QT * experts].rearrange("p (a b) -> p a b", a=QT), prod, ALU.add))
                link(red(top[:, 0:1], bank[6][:, 2 * experts:3 * experts], AX_X, ALU.max))
                cp(most[:, :], top[:, 0:1]).then_inc(s["counted"], 1)

            def make_lists(m, r):
                experts = SHAPES[m][0]
                if r == 1:
                    dve.wait_ge(s["y_free"], NB + experts_before(m, 1))
                    link(ts_(position[:, :, 0:experts], position[:, :, 0:experts], float(-P), None, ALU.add))
                dve.wait_ge(s["attn_landed"], 16)
                for qt in range(QT):
                    slots = times(slot_numbers, experts)
                    tt_(onehot_slots[:, qt, 0:experts, :], slots, over(position[:, qt, 0:experts], P), ALU.is_equal
                        ).then_inc(s["slots_marked"], 1)
                dve.wait_ge(s["listed"], 2 * m + r + 1)
                got = bank[7][:, 0:3 * experts].rearrange("p (e c) -> p e c", c=3)
                tok, pair = lists_f[:, 0:experts], lists_f[:, E1:E1 + experts]
                link(ts_(pair, got[:, :, 2], -1.0, -float(SKIP), ALU.add, ALU.mult))
                link(tt_(tok, pair, got[:, :, 0], ALU.add))
                link(stt(pair, got[:, :, 1], float(SEQ), tok, ALU.mult, ALU.add))
                link(cp(idx_token[:, 0:experts], tok))
                cp(idx_pair[:, 0:experts], pair).then_inc(s["lists"], 1)

            def route1():
                n = QT
                make_falling()
                dve.wait_ge(s["logits_made"], 1)
                ps = bank[5][:, 0:QT * (GROUPS1 + E1)].rearrange("p (a b) -> p a b", a=QT)
                lg = rt[0][:, 0:n * GROUPS1].rearrange("p (a b) -> p a b", a=n)
                le = rt[2][:, :].rearrange("p (a b) -> p a b", a=n)
                gm, pg, m1, m2, sm = (rs[i][:, 0:n] for i in range(5))
                ex = rt[1][:, 0:n * GROUPS1].rearrange("p (a b) -> p a b", a=n)
                hot = rt[3][:, 0:n * GROUPS1]
                link(cp(lg, ps[:, :, 0:GROUPS1]))
                link(cp(le, ps[:, :, GROUPS1:]))
                link(red(gm, lg, AX_X, ALU.max))
                link(first_largest(hot.rearrange("p (a b) -> p a b", a=n), lg, gm, GROUPS1))
                tt_(ex, lg, over(gm, GROUPS1), ALU.subtract).then_inc(s["route_exp_in"], 1)
                dve.wait_ge(s["route_exp"], 1)
                link(red(sm, ex, AX_X, ALU.add))
                link(nc.vector.reciprocal(pg, sm))
                off = rt[4][:, 0:n * GROUPS1]
                link(ts_(off, hot, -1.0, -NEG, ALU.add, ALU.mult))
                le4 = rt[2][:, :].rearrange("p (a b) -> p a b", b=PER1)
                link(tt_(le4, le4, over(hot, PER1), ALU.mult))
                link(tt_(le4, le4, over(off, PER1), ALU.add))
                link(red(m1, le, AX_X, ALU.max))
                top1, rest, top2 = (rt[i][:, :].rearrange("p (a b) -> p a b", a=n) for i in (6, 8, 9))
                link(first_largest(top1, le, m1, E1))
                link(stt(rest, top1, NEG, le, ALU.mult, ALU.add))
                link(red(m2, rest, AX_X, ALU.max))
                link(first_largest(top2, rest, m2, E1))
                tt_(keep[:, :, :], top1, top2, ALU.add).then_inc(s["kept"], 1)
                dve.wait_ge(s["kept"], 1)
                dif = rt[5][:, :].rearrange("p (a b) -> p a b", a=n)
                tt_(dif, le, over(m1, E1), ALU.subtract).then_inc(s["route_exp_in"], 1)
                dve.wait_ge(s["route_exp"], 2)
                link(tt_(dif, dif, keep, ALU.mult))
                link(red(sm, dif, AX_X, ALU.add))
                link(nc.vector.reciprocal(gm, sm))
                link(tt_(gm, gm, pg, ALU.mult))
                link(tt_(gate_rows[:, :, 0:E1], dif, over(gm, E1), ALU.mult))
                place_tokens(0, keep[:, :, 0:E1], gate_rows[:, :, 0:E1])

            def route2():
                n = QT
                make_falling()
                dve.wait_ge(s["logits_made"], 2)
                ps = bank[5][:, 0:n * E2].rearrange("p (a b) -> p a b", a=n)
                gm, gs = rs[0][:, 0:n], rs[1][:, 0:n]
                ex = rt[1][:, 0:n * E2]
                ex3 = ex.rearrange("p (a b) -> p a b", a=n)
                ex4 = ex.rearrange("p (a b) -> p a b", b=PER2)
                link(red(gm, ps, AX_X, ALU.max))
                tt_(ex3, ps, over(gm, E2), ALU.subtract).then_inc(s["route_exp_in"], 1)
                dve.wait_ge(s["route_exp"], 3)
                m1, m2, sm, hot = (rs[i][:, 0:n * GROUPS2] for i in range(2, 6))
                w = rt[3][:, 0:n * E2]
                w4 = w.rearrange("p (a b) -> p a b", b=PER2)
                link(red(m1, ex4, AX_X, ALU.max))
                rest, top2 = (rt[i][:, 0:n * E2].rearrange("p (a b) -> p a b", b=PER2) for i in (8, 9))
                link(first_largest(w4, ex4, m1, PER2))
                link(stt(rest, w4, -2.0, ex4, ALU.mult, ALU.add))
                link(red(m2, rest, AX_X, ALU.max))
                link(first_largest(top2, rest, m2, PER2))
                link(tt_(w4, w4, top2, ALU.add))
                link(tt_(sm, m1, m2, ALU.add))
                sm3 = sm.rearrange("p (a b) -> p a b", a=n)
                link(red(gs, sm3, AX_X, ALU.max))
                link(first_largest(hot.rearrange("p (a b) -> p a b", a=n), sm3, gs, GROUPS2))
                link(tt_(w4, w4, over(hot, PER2), ALU.mult))
                w3 = w.rearrange("p (a b) -> p a b", a=n)
                cp(keep[:, :, 0:E2], w3).then_inc(s["kept"], 1)
                link(nc.vector.reciprocal(gm, gs))
                dve.wait_ge(s["kept"], 2)
                link(tt_(w, w, ex, ALU.mult))
                link(tt_(gate_rows[:, :, 0:E2], w3, over(gm, E2), ALU.mult))
                place_tokens(1, keep[:, :, 0:E2], gate_rows[:, :, 0:E2])

            def mixture_pass(m, r):
                experts, sub, g0 = SHAPES[m]
                slices, per = experts * sub, steps_per_turn(sub)
                e_per = per // sub
                ahead = 2 if sub == 1 else 1
                eb, sb_ = experts_before(m, r), slices_before(m, r)
                make_lists(m, r)

                def hidden(t_, i):
                    dve.wait_ge(s["silu_made"], per * t_ + (sb_ + i + 1))
                    tt_(hid[i % 2], act_h[i % 2], bank[i % 2][:, FS:2 * FS], ALU.mult).then_inc(s["hid_ready"], 1)

                def copy_x(t_, e):
                    dve.wait_ge(s["x_turned"], e_per * t_ + (eb + e + 1))
                    cp(x_cols[e % NB][:, 4:8, :].rearrange("p a b -> p (a b)"), bank[4][:, :]).then_inc(s["x_copied"], 1)

                def copy_y(t_, i):
                    e = i // sub
                    if r == 0:
                        dve.wait_ge(slots_used, per * t_ + (i + 1 + g0))
                    else:
                        dve.wait_ge(used2, per * t_ + (i + 1 + m * E1 * E1_SUB))
                    dve.wait_ge(s["y_free"], e_per * t_ + (eb + e + 1))
                    cp(y_rows[e % NB][:, 512:D], bank[6][:, :]).then_inc(s["y_ready"], 1)

                def step(t_, i, last_slice):
                    if not last_slice:
                        hidden(t_, i + 1)
                    if i % sub == 0 and (not (type(t_) is int) or i // sub + ahead < experts):
                        copy_x(t_, i // sub + ahead)
                    if i % sub == sub - 1:
                        copy_y(t_, i)

                for e in range(ahead):
                    copy_x(0, e)
                hidden(0, 0)
                turns = (slices - 1) // per
                with dve.Fori(0, turns) as t_:
                    for i in range(per):
                        step(t_, i, False)
                for i in range(per * turns, slices):
                    step(0, i, i == slices - 1)

            def mixture(m):
                mixture_pass(m, 0)
                n_links = link.n
                with dve.If(overflow(dve, m)):
                    mixture_pass(m, 1)
                n = E1 * E1_SUB
                counts = [(s["dve_chain"], n_links, link.n - n_links)]
                if m == 0:
                    counts += [(s["slots_marked"], QT, QT), (s["lists"], 1, 1), (s["hid_ready"], n, n)]
                made_good(dve, m, counts)
                dve.wait_ge(s["y_loaded"], 16 * (m + 1))
                for qt in range(QT):
                    link(ts_(y_sum[:, qt, :], y_all[:, qt, :], choice_gates[:, 0, qt:qt + 1], None, ALU.mult))
                    ins = stt(y_sum[:, qt, :], y_all[:, QT + qt, :], choice_gates[:, 1, qt:qt + 1], y_sum[:, qt, :],
                              ALU.mult, ALU.add)
                    if qt < QT - 1:
                        link(ins)
                ins.then_inc(s["y_summed"], 1)
                dve.wait_ge(s["y_turned"], m + 1)

            route1()
            mixture(0)
            for j in range(KT):
                ins = stt(X[:, j, :], bank[4 + j // 2][:, (j % 2) * SEQ:(j % 2 + 1) * SEQ], mod[:, 5 * KT + j, 0:1],
                          X[:, j, :], ALU.mult, ALU.add)
                ins.then_inc(s["residual"], 1)
            dve.wait_ge(s["rnorm"], 2)
            link(tt_(X, X, times(norm_r, KT), ALU.mult))
            tt_(X, X, over(V("final_norm_g"), SEQ), ALU.mult).then_inc(s["x3_ready"], 1)

            dve.wait_ge(s["attn_landed"], 16)
            def sb_logs(a):
                dve.wait_ge(s["sb_soft"], a + 1)
                b = sc[a % 2].rearrange("p a b -> p (a b)")
                lm = sc[2 + a % 2].rearrange("p a b -> p (a b)")
                if a >= 2:
                    dve.wait_ge(s["sb_between"], a - 1)
                z = bank[Z_BANKS[a % 2]][:, :]
                link(stt(b, z, 0.0, b, ALU.min, ALU.subtract))
                link(tt_(lm, b, z, ALU.subtract))
                tt_(lm, lm, before.rearrange("p a b -> p (a b)"), ALU.mult).then_inc(s["sb_logs"], 1)

            def sb_exponent(a):
                dve.wait_ge(s["sb_between"], a + 1)
                if a >= 2:
                    dve.wait_ge(s["valued"], 2 * a - 3)
                tt_(sc[4 + a % 2].rearrange("p a b -> p (a b)"), sc[a % 2].rearrange("p a b -> p (a b)"),
                    bank[2][:, :], ALU.add).then_inc(s["sb_exponent"], 1)

            def sb_weights(a):
                dve.wait_ge(s["sb_exped"], a + 1)
                tt_(sc[4 + a % 2], sc[4 + a % 2], before, ALU.mult).then_inc(s["sb_weights"], 1)

            def take(p):
                for kind in range(2):
                    dve.wait_ge(s["valued"], 4 * p + 3 + kind)
                    cp(o_att[:, p + 4 * kind, :], bank[4 + kind][:, 0:SEQ]).then_inc(s["o_taken"], 1)

            def dl_shift(a):
                dve.wait_ge(s["scored"], 2 * a + 2)
                if a >= 1:
                    dve.wait_ge(s["dl_shifted"], a)
                link(red(am[:, 2, :], bank[SCORE_BANKS[a % 2]][:, :].rearrange("p (a b) -> p a b", a=QT), AX_X, ALU.max))
                ts_(am[:, a % 2, :], am[:, 2, :], -1.0, None, ALU.mult).then_inc(s["dl_shifted"], 1)

            def dl_probs(a):
                dve.wait_ge(s["dl_exped"], 2 * a + 2)
                if a >= 1:
                    dve.wait_ge(s["dl_probs"], a)
                if a >= 2:
                    dve.wait_ge(s["dl_turned"], a - 1)
                dst = sd[2 + a % 2]
                link(tt_(dst, sd[a % 2], count, ALU.mult))
                link(red(am[:, 2, :], dst, AX_X, ALU.add))
                link(nc.vector.reciprocal(am[:, 3, :], am[:, 2, :]))
                tt_(dst, dst, over(am[:, 3, :], SEQ), ALU.mult).then_inc(s["dl_probs"], 1)

            dve.wait_ge(s["x3_ready"], 1)
            for a in range(H2 + 1):
                if a >= 4 and a % 2 == 0:
                    take(a // 2 - 2)
                if a < H2:
                    dl_shift(a)
                if a >= 1:
                    sb_exponent(a - 1)
                    dl_probs(a - 1)
                    sb_weights(a - 1)
                if a < H2:
                    sb_logs(a)
            take(3)
            dve.wait_ge(s["o_taken"], H2)
            oa = o_att.rearrange("p a b -> p (a b)")
            tt_(sq_att.rearrange("p a b -> p (a b)"), oa, oa, ALU.mult).then_inc(s["heads_squared"], 1)
            dve.wait_ge(s["heads_rnorm"], 8)
            link(tt_(oa, oa, r_att.rearrange("p a b -> p (a b)"), ALU.mult))
            tt_(o_att, o_att, over(V("g_heads"), SEQ), ALU.mult).then_inc(s["att_normed"], 1)
            for j in range(KT):
                dve.wait_ge(s["out2_made"], j + 1)
                stt(X[:, j, :], X[:, j, :], ALPHA, bank[j % 4][:, 0:SEQ], ALU.mult, ALU.add).then_inc(s["residual"], 1)

            def layer_norm(i, name, then):
                dve.wait_ge(s["ln_mean_copied"], i + 1)
                tt_(X, X, times(norm_m, KT), ALU.subtract).then_inc(s["ln_centred"], 1)
                dve.wait_ge(s["ln_centred"], i + 1)
                dve.wait_ge(s["ln_rnorm"], i + 1)
                link(tt_(X, X, times(norm_r, KT), ALU.mult))
                for k in range(KT):
                    ts_(X[:, k, :], X[:, k, :], V(name + "_g")[:, k:k + 1], V(name + "_b")[:, k:k + 1], ALU.mult, ALU.add
                        ).then_inc(s[then], 1)

            layer_norm(0, "ln1", "route_in1")
            route2()
            mixture(1)
            for j in range(KT):
                stt(X[:, j, :], X[:, j, :], ALPHA, bank[4 + j // 2][:, (j % 2) * SEQ:(j % 2 + 1) * SEQ],
                    ALU.mult, ALU.add).then_inc(s["residual"], 1)
            layer_norm(1, "ln2", "ln2_done")


def by_partition(w):
    return w.reshape(-1, P, w.shape[-1]).transpose(1, 0, 2)


def as_block(w, col):
    return by_partition(w[:, col:col + P]).reshape(P, D)


def lay_out(a):
    a = {k: np.asarray(v) for k, v in a.items()}
    w_in, w_in2 = a["w_in"][0], a["w_in_2"][0]
    col_ba = 3 * D
    col_z = col_ba + 4 * HEADS
    col_u, col_v, col_g = col_z + D, col_z + 2 * D, col_z + 3 * D
    stream = np.zeros((N_GROUPS, P, GROUP), np.float32)

    def put(first_group, j, block):
        at = (j % BLOCKS) * D
        stream[first_group + j // BLOCKS, :, at:at + D] = block

    for j in range(6 * KT):
        put(0, ADA0 + j, as_block(a["ada_w"][0], j * P))
    for j in range(KT):
        put(0, V0 + j, as_block(w_in, col_v + j * P))
        put(0, U0 + j, as_block(w_in, col_u + j * P))
        put(0, Z0 + j, as_block(w_in, col_z + j * P))
        put(0, G0 + 2 * j, as_block(w_in, col_g + j * P))
        put(0, G0 + 2 * j + 1, as_block(w_in, col_g + D + j * P))
        put(0, AB0 + 2 * j, as_block(a["w_branch_a"][0], j * P))
        put(0, AB0 + 2 * j + 1, as_block(a["w_branch_b"][0], j * P))
        put(0, O0 + j, as_block(a["w_out"][0], j * P))
        put(SECOND_G, O20 + j, as_block(a["w_out_2"][0], j * P))
    for j in range(O20):
        put(SECOND_G, j, as_block(w_in2, j * P))

    def experts(first_group, n, sub, w1, w3, w2):
        for e in range(n):
            for i in range(sub):
                f = slice(i * FS, (i + 1) * FS)
                dst = stream[first_group + e * sub + i]
                both = np.concatenate([by_partition(w1[e][:, f]), by_partition(w3[e][:, f])], 2)
                dst[:, 0:2 * KT * FS] = both.reshape(P, -1)
                dst[:, 2 * KT * FS:] = by_partition(w2[e][f]).reshape(P, -1)

    experts(MOE1_G, E1, E1_SUB, a["expert_w1"][0], a["expert_w3"][0], a["expert_w2"][0])
    experts(MOE2_G, E2, E2_SUB, a["w_gate_2"][0], a["w_up_2"][0], a["w_down_2"][0])

    head_w = np.zeros((HEADS + 1, P, 3 * D), np.float32)
    for h in range(HEADS):
        for j in range(3):
            head_w[h, :, j * D:(j + 1) * D] = as_block(w_in, j * D + h * P)
    head_w[HEADS, :, 0:D] = a["sgu_ln_g"][0][None, :]
    head_w[HEADS, :, D:2 * D] = a["sgu_ln_b"][0][None, :]
    head_w[HEADS, :, 2 * D:] = a["sgu_w"][0].transpose(2, 0, 1).reshape(P, D)

    vec = np.zeros((P, VEC_N), np.float32)

    def cols(v):
        return v.reshape(-1, P).T
    vec[:, VEC["cond"]] = np.stack([cols(a["c"][0]), cols(a["c_ctx"])], 2).reshape(P, -1)
    vec[:, VEC["ada_b"]] = cols(a["ada_b"][0])
    for name in ("norm_mix_g", "gdn_norm_g", "norm_ffn_g"):
        vec[:, VEC[name]] = cols(a[name][0])
    vec[:, VEC["final_norm_g"]] = cols(a["final_norm_g"])
    for name in ("ln1_g", "ln1_b", "ln2_g", "ln2_b"):
        vec[:, VEC[name]] = cols(a[name + "_2"][0])
    vec[:, VEC["g_heads"]] = cols(np.concatenate([a["g_sb_2"][0], a["g_dil_2"][0]]))
    vec[:, VEC["conv_w"]] = a["conv_w"][0].reshape(CONV, 3, HEADS, P).transpose(3, 2, 1, 0).reshape(P, -1)
    vec[:, VEC["token"]] = np.arange(SEQ).reshape(QT, P).T
    vec[:, VEC["dt_bias"]] = a["dt_bias"][0].reshape(1, DH)
    vec[:, VEC["a_log"]] = a["a_log"][0].reshape(1, DH)

    xc = np.concatenate([by_partition(a["ctx"][0].T), by_partition(a["x"][0].T)], 2)
    rows = np.concatenate([a["sgu_b"][0].reshape(-1), a["router_group_b"][0], a["router_expert_b"][0], a["b_router_2"]])
    router1 = np.concatenate([by_partition(a["router_group_w"][0]), by_partition(a["router_expert_w"][0])], 2)
    router_w = np.concatenate([router1.reshape(P, -1), by_partition(a["w_router_2"]).reshape(P, -1)], 1)
    square, attn, onehot = shape_constants()
    return {
        "stream": stream, "head_w": head_w, "vec": vec, "xc": xc, "rows": rows[None, :], "router_w": router_w,
        "ba_w": by_partition(w_in[:, col_ba:col_z]), "square": square, "attn": attn, "onehot": onehot,
        "rel_bias": a["rel_bias_2"],
    }


def kernel(**inputs):
    import concourse.bacc as bacc
    from concourse.bass_utils import run_bass_kernel_spmd

    nc = bacc.Bacc("TRN2", target_bir_lowering=False, num_devices=1)
    arrays = {f"in_{k}": np.ascontiguousarray(v) for k, v in lay_out(inputs).items()}
    t = {k[3:]: nc.dram_tensor(k, v.shape, F32, kind="ExternalInput").ap() for k, v in arrays.items()}
    t["out"] = nc.dram_tensor("out_y", (P, KT, SEQ), F32, kind="ExternalOutput").ap()
    build(nc, t)
    got = run_bass_kernel_spmd(nc, [arrays], core_ids=[0]).results[0]["out_y"]
    return np.ascontiguousarray(np.asarray(got).transpose(2, 1, 0).reshape(1, SEQ, D))
```
